# Optimizing a Trainium2 kernel written in Bass

```python
import jax, jax.numpy as jnp
from jax import lax
import numpy as np

D_MODEL = 1024
BATCH = 1
SEQ = 1024
DEPTH = 4
DEC_BATCH = 8
DEC_SEQ = 1
PAST_LEN = 1024
PAGE_SIZE = 128

N_MIXERS = 3
N_LAYERS_A = (DEPTH + 2) // 3
N_LAYERS_B = (DEPTH + 1) // 3
N_LAYERS_C = DEPTH // 3
NORM_EPS = 1e-6
LN_EPS = 1e-5

A_EXPAND = 2
D_A = A_EXPAND * D_MODEL
CHUNK = 128
A_GROUPS = 4

HEAD_DIM = 64
N_HEADS = D_MODEL // HEAD_DIM
N_KV_HEADS = N_HEADS // 8
Q_PER_KV = N_HEADS // N_KV_HEADS
WINDOW = 128
ROPE_THETA = 10000.0

D_RNN = D_MODEL
C_BLOCKS = 4
C_BLOCK_W = D_RNN // C_BLOCKS
CONV_W = 4
LRU_C = 8.0

kernel_name = 'hybrid_gmlp_swa_rglru_decode_step'

def rms_norm(x, g):
    xf = x.astype(jnp.float32)
    y = xf * lax.rsqrt(jnp.mean(xf * xf, axis=-1, keepdims=True) + NORM_EPS)
    return (y * g.astype(jnp.float32)).astype(x.dtype)

def layer_norm(x, g, b):
    xf = x.astype(jnp.float32)
    mu = jnp.mean(xf, axis=-1, keepdims=True)
    var = jnp.mean(jnp.square(xf - mu), axis=-1, keepdims=True)
    y = (xf - mu) * lax.rsqrt(var + LN_EPS)
    return (y * g.astype(jnp.float32) + b.astype(jnp.float32)).astype(x.dtype)

def rope(x, pos):
    half = HEAD_DIM // 2
    inv_freq = ROPE_THETA ** (-jnp.arange(half, dtype=jnp.float32) / half)
    ang = pos.astype(jnp.float32)[:, None] * inv_freq[None, :]
    cos = jnp.cos(ang)[:, None, :]
    sin = jnp.sin(ang)[:, None, :]
    xf = x.astype(jnp.float32)
    x1, x2 = xf[..., :half], xf[..., half:]
    return jnp.concatenate([x1 * cos - x2 * sin, x2 * cos + x1 * sin], axis=-1).astype(x.dtype)

def sink_softmax(scores, mask, sinks):
    s = jnp.where(mask, scores.astype(jnp.float32), -jnp.inf)
    sink = sinks.astype(jnp.float32)[..., None, None]
    m = jnp.maximum(jnp.max(s, axis=-1, keepdims=True), sink)
    e = jnp.exp(s - m)
    return e / (jnp.sum(e, axis=-1, keepdims=True) + jnp.exp(sink - m))

def mixer_a(h, w_in, ln_g, ln_b, w_s, b_s, w_out):
    bsz, t_len, _ = h.shape
    u, v, g = jnp.split(h @ w_in, 3, axis=-1)
    u = jax.nn.gelu(u)
    v = layer_norm(jax.nn.gelu(v), ln_g, ln_b)
    n_chunks = -(-t_len // CHUNK)
    pad = n_chunks * CHUNK - t_len
    vc = jnp.pad(v, ((0, 0), (0, pad), (0, 0))).reshape(bsz, n_chunks, CHUNK, A_GROUPS, D_A // A_GROUPS)
    causal = jnp.tril(jnp.ones((CHUNK, CHUNK), dtype=bool))
    ws = jnp.where(causal[None], w_s, 0.0)
    mixed = jnp.einsum('gts,bnsgc->bntgc', ws, vc) + b_s.T[None, None, :, :, None]
    mixed = mixed.reshape(bsz, n_chunks * CHUNK, D_A)[:, :t_len]
    out = (u * mixed * jax.nn.silu(g)) @ w_out
    return out, v

def project_b(h, w_in):
    bsz, t_len, _ = h.shape
    qd, kd = N_HEADS * HEAD_DIM, N_KV_HEADS * HEAD_DIM
    z = h @ w_in
    q = z[..., :qd].reshape(bsz, t_len, N_HEADS, HEAD_DIM)
    k = z[..., qd:qd + kd].reshape(bsz, t_len, N_KV_HEADS, HEAD_DIM)
    v = z[..., qd + kd:qd + 2 * kd].reshape(bsz, t_len, N_KV_HEADS, HEAD_DIM)
    g = z[..., qd + 2 * kd:]
    return q, k, v, g

def mixer_b_prompt(h, w_in, sinks, w_out):
    bsz, t_len, _ = h.shape
    q, k, v, g = project_b(h, w_in)
    pos = jnp.arange(t_len, dtype=jnp.int32)
    q, k = rope(q, pos), rope(k, pos)
    nb = t_len // WINDOW
    qb = q.reshape(bsz, nb, WINDOW, N_KV_HEADS, Q_PER_KV, HEAD_DIM)
    kb = k.reshape(bsz, nb, WINDOW, N_KV_HEADS, HEAD_DIM)
    vb = v.reshape(bsz, nb, WINDOW, N_KV_HEADS, HEAD_DIM)
    prev = lambda a: jnp.pad(a, ((0, 0), (1, 0), (0, 0), (0, 0), (0, 0)))[:, :-1]
    kk = jnp.concatenate([prev(kb), kb], axis=2)
    vv = jnp.concatenate([prev(vb), vb], axis=2)
    scores = jnp.einsum('bnqkgd,bnskd->bnkgqs', qb, kk) * (HEAD_DIM ** -0.5)
    blk = jnp.arange(nb)[:, None, None]
    qpos = blk * WINDOW + jnp.arange(WINDOW)[None, :, None]
    kpos = (blk - 1) * WINDOW + jnp.arange(2 * WINDOW)[None, None, :]
    mask = (kpos <= qpos) & (qpos - kpos <= WINDOW) & (kpos >= 0)
    p = sink_softmax(scores, mask[None, :, None, None], sinks.reshape(N_KV_HEADS, Q_PER_KV))
    o = jnp.einsum('bnkgqs,bnskd->bnqkgd', p.astype(vv.dtype), vv).reshape(bsz, t_len, N_HEADS * HEAD_DIM)
    out = (o * jax.nn.silu(g)) @ w_out
    keep = min(WINDOW, t_len)
    return out, k[:, t_len - keep:], v[:, t_len - keep:]

def mixer_b_sample(h, buf_k, buf_v, w_in, sinks, w_out):
    bsz, t_len, _ = h.shape
    wb = buf_k.shape[1]
    q, k, v, g = project_b(h, w_in)
    qpos = PAST_LEN + jnp.arange(t_len, dtype=jnp.int32)
    q, k = rope(q, qpos), rope(k, qpos)
    kk = jnp.concatenate([buf_k.astype(k.dtype), k], axis=1)
    vv = jnp.concatenate([buf_v.astype(v.dtype), v], axis=1)
    kpos = jnp.concatenate([PAST_LEN - wb + jnp.arange(wb, dtype=jnp.int32), qpos])
    qg = q.reshape(bsz, t_len, N_KV_HEADS, Q_PER_KV, HEAD_DIM)
    scores = jnp.einsum('btkgd,bskd->bkgts', qg, kk) * (HEAD_DIM ** -0.5)
    mask = (kpos[None, :] <= qpos[:, None]) & (qpos[:, None] - kpos[None, :] <= WINDOW)
    p = sink_softmax(scores, mask, sinks.reshape(N_KV_HEADS, Q_PER_KV))
    o = jnp.einsum('bkgts,bskd->btkgd', p.astype(vv.dtype), vv).reshape(bsz, t_len, N_HEADS * HEAD_DIM)
    out = (o * jax.nn.silu(g)) @ w_out
    keep = min(WINDOW, wb + t_len)
    return out, kk[:, wb + t_len - keep:], vv[:, wb + t_len - keep:]

def mixer_c(h, conv_buf, h0, pos, w_in, conv_w, conv_b, w_a, b_a, w_x, b_x, lam, w_out):
    bsz, t_len, _ = h.shape
    xr, g = jnp.split(h @ w_in, 2, axis=-1)
    xpad = jnp.concatenate([conv_buf.astype(xr.dtype), xr], axis=1)
    xc = conv_b + xpad[:, 0:t_len] * conv_w[0]
    for tap in range(1, CONV_W):
        xc = xc + xpad[:, tap:tap + t_len] * conv_w[tap]
    new_conv = xpad[:, t_len:]
    xblk = xc.reshape(bsz, t_len, C_BLOCKS, C_BLOCK_W)
    r = jax.nn.sigmoid(jnp.einsum('btnc,ncd->btnd', xblk, w_a).reshape(bsz, t_len, D_RNN) + b_a)
    i_gate = jax.nn.sigmoid(jnp.einsum('btnc,ncd->btnd', xblk, w_x).reshape(bsz, t_len, D_RNN) + b_x)
    log_a = -LRU_C * r.astype(jnp.float32) * jax.nn.softplus(-lam.astype(jnp.float32))
    a = jnp.exp(log_a)
    mult = jnp.sqrt(-jnp.expm1(2.0 * log_a))
    mult = jnp.where((pos == 0)[None, :, None], 1.0, mult)
    bterm = mult * (i_gate * xc).astype(jnp.float32)
    bterm = bterm.at[:, 0].add(a[:, 0] * h0.astype(jnp.float32))

    def combine(left, right):
        a1, b1 = left
        a2, b2 = right
        return a1 * a2, a2 * b1 + b2

    _, hs = lax.associative_scan(combine, (a, bterm), axis=1)
    out = (hs.astype(h.dtype) * jax.nn.silu(g)) @ w_out
    return out, new_conv, hs[:, -1]

def setup_inputs(seed: int = 0) -> dict:
    key = jax.random.key(seed)
    ks = jax.random.split(key, 32)
    f32 = jnp.float32

    def nrm(k, shape, scale):
        return jax.random.normal(k, shape, f32) * scale

    w_buf = min(WINDOW, PAST_LEN)
    qkvg = 2 * N_HEADS * HEAD_DIM + 2 * N_KV_HEADS * HEAD_DIM
    u = jax.random.uniform(ks[29], (N_LAYERS_C, D_RNN), f32, 0.9, 0.999)
    base = u ** (1.0 / LRU_C)
    c_lam = jnp.log(base) - jnp.log1p(-base)
    return {
        'x_prompt': nrm(ks[0], (BATCH, SEQ, D_MODEL), 1.0),
        'x_sample': nrm(ks[1], (DEC_BATCH, DEC_SEQ, D_MODEL), 1.0),
        'cache_b_k': nrm(ks[2], (N_LAYERS_B, DEC_BATCH, w_buf, N_KV_HEADS, HEAD_DIM), 1.0),
        'cache_b_v': nrm(ks[3], (N_LAYERS_B, DEC_BATCH, w_buf, N_KV_HEADS, HEAD_DIM), 1.0),
        'state_c_conv': nrm(ks[4], (N_LAYERS_C, DEC_BATCH, CONV_W - 1, D_RNN), 1.0),
        'state_c_h': nrm(ks[5], (N_LAYERS_C, DEC_BATCH, D_RNN), 0.5),
        'norm_pre': 1.0 + nrm(ks[6], (DEPTH, D_MODEL), 0.02),
        'norm_post': 1.0 + nrm(ks[7], (DEPTH, D_MODEL), 0.02),
        'a_w_in': nrm(ks[8], (N_LAYERS_A, D_MODEL, 3 * D_A), D_MODEL ** -0.5),
        'a_ln_g': 1.0 + nrm(ks[9], (N_LAYERS_A, D_A), 0.02),
        'a_ln_b': nrm(ks[10], (N_LAYERS_A, D_A), 0.02),
        'a_w_s': nrm(ks[11], (N_LAYERS_A, A_GROUPS, CHUNK, CHUNK), CHUNK ** -0.5),
        'a_b_s': 1.0 + nrm(ks[12], (N_LAYERS_A, A_GROUPS, CHUNK), 0.02),
        'a_w_out': nrm(ks[13], (N_LAYERS_A, D_A, D_MODEL), D_A ** -0.5),
        'b_w_in': nrm(ks[14], (N_LAYERS_B, D_MODEL, qkvg), D_MODEL ** -0.5),
        'b_sinks': nrm(ks[15], (N_LAYERS_B, N_HEADS), 1.0),
        'b_w_out': nrm(ks[16], (N_LAYERS_B, N_HEADS * HEAD_DIM, D_MODEL), (N_HEADS * HEAD_DIM) ** -0.5),
        'c_w_in': nrm(ks[17], (N_LAYERS_C, D_MODEL, 2 * D_RNN), D_MODEL ** -0.5),
        'c_conv_w': nrm(ks[18], (N_LAYERS_C, CONV_W, D_RNN), CONV_W ** -0.5),
        'c_conv_b': nrm(ks[19], (N_LAYERS_C, D_RNN), 0.02),
        'c_w_a': nrm(ks[20], (N_LAYERS_C, C_BLOCKS, C_BLOCK_W, C_BLOCK_W), C_BLOCK_W ** -0.5),
        'c_b_a': nrm(ks[21], (N_LAYERS_C, D_RNN), 0.02),
        'c_w_x': nrm(ks[22], (N_LAYERS_C, C_BLOCKS, C_BLOCK_W, C_BLOCK_W), C_BLOCK_W ** -0.5),
        'c_b_x': nrm(ks[23], (N_LAYERS_C, D_RNN), 0.02),
        'c_lam': c_lam,
        'c_w_out': nrm(ks[24], (N_LAYERS_C, D_RNN, D_MODEL), D_RNN ** -0.5),
    }

def reference(x_prompt, x_sample, cache_b_k, cache_b_v, state_c_conv, state_c_h,
              norm_pre, norm_post,
              a_w_in, a_ln_g, a_ln_b, a_w_s, a_b_s, a_w_out,
              b_w_in, b_sinks, b_w_out,
              c_w_in, c_conv_w, c_conv_b, c_w_a, c_b_a, c_w_x, c_b_x, c_lam, c_w_out):
    xp, xs = x_prompt, x_sample
    pos_p = jnp.arange(xp.shape[1], dtype=jnp.int32)
    pos_s = PAST_LEN + jnp.arange(xs.shape[1], dtype=jnp.int32)
    a_v_s = []
    b_kp, b_vp, b_ks, b_vs = [], [], [], []
    c_cp, c_hp, c_cs, c_hs = [], [], [], []
    for i in range(DEPTH):
        kind, j = i % N_MIXERS, i // N_MIXERS
        hp = rms_norm(xp, norm_pre[i])
        hs = rms_norm(xs, norm_pre[i])
        if kind == 0:
            yp, _ = mixer_a(hp, a_w_in[j], a_ln_g[j], a_ln_b[j], a_w_s[j], a_b_s[j], a_w_out[j])
            ys, vs = mixer_a(hs, a_w_in[j], a_ln_g[j], a_ln_b[j], a_w_s[j], a_b_s[j], a_w_out[j])
            a_v_s.append(vs)
        elif kind == 1:
            yp, kp, vp = mixer_b_prompt(hp, b_w_in[j], b_sinks[j], b_w_out[j])
            ys, ks_, vs_ = mixer_b_sample(hs, cache_b_k[j], cache_b_v[j], b_w_in[j], b_sinks[j], b_w_out[j])
            b_kp.append(kp); b_vp.append(vp); b_ks.append(ks_); b_vs.append(vs_)
        else:
            yp, cp, hlp = mixer_c(hp, jnp.zeros((hp.shape[0], CONV_W - 1, D_RNN), hp.dtype),
                                  jnp.zeros((hp.shape[0], D_RNN), jnp.float32), pos_p,
                                  c_w_in[j], c_conv_w[j], c_conv_b[j], c_w_a[j], c_b_a[j],
                                  c_w_x[j], c_b_x[j], c_lam[j], c_w_out[j])
            ys, cs, hls = mixer_c(hs, state_c_conv[j], state_c_h[j], pos_s,
                                  c_w_in[j], c_conv_w[j], c_conv_b[j], c_w_a[j], c_b_a[j],
                                  c_w_x[j], c_b_x[j], c_lam[j], c_w_out[j])
            c_cp.append(cp); c_hp.append(hlp); c_cs.append(cs); c_hs.append(hls)
        xp = xp + rms_norm(yp, norm_post[i])
        xs = xs + rms_norm(ys, norm_post[i])
    new_a_v_sample = jnp.stack(a_v_s)
    new_b_k_prompt = jnp.stack(b_kp)
    new_b_v_prompt = jnp.stack(b_vp)
    new_b_k_sample = jnp.stack(b_ks)
    new_b_v_sample = jnp.stack(b_vs)
    new_c_conv_prompt = jnp.stack(c_cp)
    new_c_h_prompt = jnp.stack(c_hp)
    new_c_conv_sample = jnp.stack(c_cs)
    new_c_h_sample = jnp.stack(c_hs)
    return (xp, xs, new_a_v_sample, new_b_k_prompt, new_b_v_prompt, new_b_k_sample, new_b_v_sample,
            new_c_conv_prompt, new_c_h_prompt, new_c_conv_sample, new_c_h_sample)


_drawn_inputs = setup_inputs


def setup_inputs(seed=0):
    import zlib

    import numpy as np

    out = dict(_drawn_inputs(seed))
    spreads = {}
    factors = {'a_ln_g': 2.811,
     'a_ln_b': 2.839,
     'a_b_s': 3.085,
     'b_sinks': 3.856,
     'c_b_a': 8.0,
     'c_b_x': 7.028}
    for name, (base, spread) in spreads.items():
        noise = np.random.default_rng([zlib.crc32(name.encode()), seed]).standard_normal(out[name].shape)
        drawn = base * np.exp(spread * noise) if base else spread * noise
        out[name] = __import__('jax').numpy.asarray(drawn.astype(out[name].dtype))
    for name, factor in factors.items():
        out[name] = (out[name] * factor).astype(out[name].dtype)
    return out
```

```python
from contextlib import ExitStack

import numpy as np

import concourse.bass as bass
from concourse import mybir

F32 = mybir.dt.float32
F32R = mybir.dt.float32r
ALU = mybir.AluOpType
ACT = mybir.ActivationFunctionType
AX = mybir.AxisListType

P = 128
D = 1024
KT = D // P
T = 1024
NS = 8
NT = T + NS
CH = 3
CW = NT // CH
TILE = NT * 4
DA = 2048
MA = DA // P
NH, HD, NKV = 16, 64, 2
WIN = 128
NBLK = T // WIN
CONV = 4
NEG = -1e30
SCALE = HD ** -0.5
N_UNITS = (3 * MA + 2 * KT) * 2 + (2 * KT + 2 + KT) + (2 * KT + 4 + KT)


class Counts:

    def __init__(self):
        self.unit = 0
        self.result = 0

    def take(self, units, results):
        at = self.unit, self.result
        self.unit += units
        self.result += results
        return at


class Signal:

    def __init__(self, sem, base):
        self.sem, self.base = sem, base

    def at(self, n):
        return self.sem, n + self.base


PER_LAYER = {
    "hi_done": (KT, KT, KT), "h_done": (KT, KT, KT), "sq_done": (KT, KT, KT), "sq_used": (KT - 2, KT - 2, KT - 2),
    "ssq_mm": (2, 2, 2), "root": (2, 2, 2), "rx_done": (1, 1, 1),
    "x_saved": (16 * KT,) * 3, "x_back": (16 * KT,) * 3, "in_done": (3 * MA, 2 * KT + 2, KT), "act_done": (MA, KT, 0),
    "y_hi_done": (0, 0, KT), "y_lo_done": (MA, 1, KT), "acc_done": (KT, 0, 0), "ysq_done": (KT, KT, KT),
    "yssq_done": (KT, KT, KT), "yssq_mm": (2, 2, 2), "yroot": (2, 2, 2), "x_new": (KT, KT, KT),
    "rp_done": (1, 1, 1), "scaled": (KT - 1,) * 3,
    "ws_in": (64, 0, 0), "wm": (1, 0, 0), "wh": (1, 0, 0), "ws_done": (1, 0, 0), "vsq": (MA, 0, 0),
    "vsum_done": (2 * MA, 0, 0), "stat_mm": (4, 0, 0), "stat": (5, 0, 0), "vst": (MA, 0, 0), "vT": (MA, 0, 0),
    "vTh": (MA, 0, 0), "vTl": (MA, 0, 0), "mix": (MA, 0, 0), "y_done": (MA, 0, KT), "u_act": (MA, 0, 0),
    "g_act": (MA, 0, KT), "tmp_hi": (MA, 0, 0), "lo_cut": (MA, 0, 0), "vout": (16, 0, 0), "var_done": (1, 0, 0),
}


def build(nc, io):
    with ExitStack() as ctx:
        def sem(name):
            return ctx.enter_context(nc.semaphore(name))

        base = (nc.sbuf_base + 31) // 32 * 32
        W_AT = base
        X_AT = W_AT + 3 * 2 * 4096
        R_AT = [X_AT + KT * TILE, X_AT + KT * TILE + MA * TILE]
        S_AT = R_AT[1] + MA * TILE
        END = nc.sbuf_usable_end

        def at(name, offset, shape, dtype=F32):
            size = 4
            for n in shape[1:]:
                size *= n
            assert offset + size <= END, (name, offset + size - END)
            return nc.alloc_sbuf_tensor_at(name, shape, dtype, offset=offset)

        small = [S_AT]

        def keep(name, shape, dtype=F32):
            size = 4
            for n in shape[1:]:
                size *= n
            o = small[0]
            small[0] += (size + 31) // 32 * 32
            return at(name, o, shape, dtype)

        w_raw = at("w_raw", W_AT, [P, 2, 8, P])
        w_hi = at("w_hi", W_AT + 8192, [P, 2, 8, P], F32R)
        w_lo = at("w_lo", W_AT + 16384, [P, 2, 8, P], F32R)
        x = at("x", X_AT, [P, KT, NT])
        rx = keep("rx", [P, NT])
        sq_at = small[0]
        sqt = keep("sqt", [P, NT])
        ssq = keep("ssq", [P, NT])
        sq2 = at("sq2", sq_at, [P, 2, NT])
        vt_hi = at("vt_hi", sq_at, [P, NBLK, P], F32R)
        vt_lo = at("vt_lo", sq_at + TILE, [P, NBLK, P], F32R)
        ident = keep("ident", [P, P])
        ones = keep("ones", [P, P])
        zero = keep("zero", [P, 8])
        g_pre = keep("g_pre", [P, 4, KT])
        g_post = keep("g_post", [P, 4, KT])
        ln_g = keep("ln_g", [P, 2, MA])
        ln_b = keep("ln_b", [P, 2, MA])
        cvec = keep("cvec", [P, 8, KT])
        eps = keep("eps", [P, 2])
        cell_act, cell_dve = keep("cell_act", [P, 8]), keep("cell_dve", [P, 8])
        v_new = keep("v_new", [P, MA, NS])
        bs_bc = keep("bs_bc", [P, 4, P])
        corner = keep("corner", [P, 4])
        ps = ctx.enter_context(nc.psum_tensor("ps", [P, 8, 512], F32))

        w_loaded = [sem("w_loaded0"), sem("w_loaded1")]
        w_hi_done, w_lo_done = sem("w_hi_done"), sem("w_lo_done")
        result = sem("result")
        evac = [sem("evac0"), sem("evac1")]
        consts = sem("consts")
        setup = sem("setup")
        x_in = [sem(f"x_in{k}") for k in range(KT)]
        n_consts = 6
        c = Counts()

        class Layer:
            pass

        layers = []
        shared = {}
        for i, kind in enumerate("abca"):
            L = Layer()
            L.i, L.kind, L.j = i, kind, i // 3
            hreg = [0, 1, 0, 1][i]
            H_AT, O_AT = R_AT[hreg], R_AT[1 - hreg]
            n = f"l{i}_"

            def s(name, i=i, kind=kind):
                if name not in shared:
                    shared[name] = sem(name)
                before = sum(PER_LAYER[name]["abc".index(k)] for k in "abca"[:i]) if name in PER_LAYER else 0
                return Signal(shared[name], before)

            L.h_hi = at(n + "h_hi", H_AT, [P, KT, NT], F32R)
            L.h_lo = at(n + "h_lo", H_AT + KT * TILE, [P, KT, NT], F32R)
            L.hi_done, L.h_done, L.sq_done = s("hi_done"), s("h_done"), s("sq_done")
            L.sq_used, L.ssq_mm, L.root, L.rx_done = s("sq_used"), s("ssq_mm"), s("root"), s("rx_done")
            L.rp_done, L.scaled = s("rp_done"), s("scaled")
            L.x_saved, L.x_back = s("x_saved"), s("x_back")
            L.in_done, L.act_done = s("in_done"), s("act_done")
            L.y_hi_done, L.y_lo_done = s("y_hi_done"), s("y_lo_done")
            L.acc_done, L.ysq_done, L.yssq_done = s("acc_done"), s("ysq_done"), s("yssq_done")
            L.yssq_mm, L.yroot, L.x_new = s("yssq_mm"), s("yroot"), s("x_new")
            if kind == "a":
                L.u0, L.r0 = c.take(3 * MA + 2 * KT, 3 * MA + 2 * KT)
                L.v = at(n + "v", O_AT, [P, MA, NT])
                L.y = L.v
                L.y_hi = at(n + "y_hi", O_AT, [P, MA, NT], F32R)
                L.y_lo = at(n + "y_lo", H_AT, [P, KT, NT], F32R)
                L.acc = at(n + "acc", H_AT + KT * TILE, [P, KT, NT])
                L.tmp = at(n + "tmp", X_AT, [P, 2, NT])
                L.ug = at(n + "ug", X_AT + 2 * TILE, [P, NT])
                L.vstage = at(n + "vstage", X_AT + 3 * TILE, [P, NT])
                L.mu = at(n + "mu", X_AT + 4 * TILE, [P, NT])
                L.rstd = at(n + "rstd", X_AT + 5 * TILE, [P, NT])
                L.vsum = at(n + "vsum", X_AT + 6 * TILE, [P, NT])
                L.wsr = at(n + "wsr", X_AT + 2 * TILE, [P, 4, P])
                L.tri = at(n + "tri", X_AT + 3 * TILE, [P, P])
                L.ws_hi = at(n + "ws_hi", X_AT + 7 * TILE, [P, 4, P], F32R)
                L.ws_lo = at(n + "ws_lo", X_AT + 7 * TILE + 2048, [P, 4, P], F32R)
                L.y_tmp = at(n + "y_tmp", X_AT, [P, 2, NT], F32R)
                L.ws_in, L.wm, L.wh, L.ws_done = s("ws_in"), s("wm"), s("wh"), s("ws_done")
                L.vsq, L.vsum_done = s("vsq"), s("vsum_done")
                L.stat_mm, L.stat = s("stat_mm"), s("stat")
                L.vst, L.vT, L.vTh, L.vTl, L.mix, L.y_done = (
                    s("vst"), s("vT"), s("vTh"), s("vTl"), s("mix"), s("y_done"))
                L.u_act, L.g_act = s("u_act"), s("g_act")
                L.tmp_hi, L.lo_cut = s("tmp_hi"), s("lo_cut")
                L.vout, L.var_done = s("vout"), s("var_done")
            if kind == "b":
                L.u0, L.r0 = c.take(2 * KT + 2 + KT, 2 * KT + 2 + KT)
                L.q = at(n + "q", O_AT, [P, KT, NT])
                L.gate = at(n + "gate", O_AT + KT * TILE, [P, KT, NT])
                L.vf = at(n + "vf", O_AT + KT * TILE, [P, NT])
                L.y_hi = at(n + "y_hi", O_AT, [P, KT, NT], F32R)
                L.y_lo = at(n + "y_lo", O_AT + KT * TILE, [P, KT, NT], F32R)
                L.acc = at(n + "acc", H_AT, [P, KT, NT])
                o = X_AT
                L.kd = at(n + "kd", o, [P, 2, P + NT]); o += 2 * (P + NT) * 4
                L.vtok = at(n + "vtok", o, [P, NBLK + 1, P]); o += (NBLK + 1) * P * 4
                L.cos = at(n + "cos", o, [P, NT]); o += TILE
                L.sin = at(n + "sin", o, [P, NT]); o += TILE
                L.kf = at(n + "kf", o, [P, NT]); o += TILE
                L.sw = at(n + "sw", o, [P, NT]); o += TILE
                L.vfs = at(n + "vfs", o, [P, 2 * NS]); o += 64
                L.v16 = at(n + "v16", o, [P, P]); o += 512
                L.sink = at(n + "sink", o, [P, NH]); o += 64
                assert o <= X_AT + KT * TILE
                o = H_AT
                L.qs = at(n + "qs", o, [P, 2, 4, P]); o += 4096
                L.vs = at(n + "vs", o, [P, 2, 2, P]); o += 2048
                L.sc = at(n + "sc", o, [P, 2, 4, 2 * WIN]); o += 8192
                L.pt = at(n + "pt", o, [P, 2, 2, 4 * P]); o += 8192
                L.yt = at(n + "yt", o, [P, 2, 2, P]); o += 2048
                L.mask = at(n + "mask", o, [P, 2, 2 * WIN]); o += 2048
                L.mx = at(n + "mx", o, [P, 2, 4, 4]); o += 128
                L.rq = at(n + "rq", o, [P, 2, 4]); o += 32
                L.kc = at(n + "kc", o, [P, 2, NS, WIN + 1]); o += 2 * NS * (WIN + 1) * 4
                L.vc = at(n + "vc", o, [P, NS, P]); o += 4096
                L.qz = at(n + "qz", o, [P, NS, NH]); o += 512
                L.ss = at(n + "ss", o, [P, 2 * NS, WIN + 1]); o += 2 * NS * (WIN + 1) * 4
                L.sk = at(n + "sk", o, [P, 2 * NS]); o += 64
                L.sm = at(n + "sm", o, [P, 5, 2 * NS]); o += 320
                L.pts = at(n + "pts", o, [P, P]); o += 512
                L.po = at(n + "po", o, [P, NS]); o += 32
                L.dx = at(n + "dx", o, [P, 2 * NS, NS]); o += 512
                L.zo = at(n + "zo", o, [P, 2 * NS, NS]); o += 512
                L.ys = at(n + "ys", o, [P, KT, NS]); o += 256
                assert o <= H_AT + MA * TILE
                L.Rq, L.rope_in, L.sw_done, L.k_rot, L.vf_done, L.v_tr = s("Rq"), s("rope_in"), s("sw_done"), s("k_rot"), s("vf_done"), s("v_tr")
                L.vfs_done, L.vtok_done, L.kout, L.at_in, L.stq, L.stv = s("vfs_done"), s("vtok_done"), s("kout"), s("at_in"), s("stq"), s("stv")
                L.S, L.B, L.X, L.C, L.TP, L.PC = s("S"), s("B"), s("X"), s("C"), s("TP"), s("PC")
                L.PV, L.Dy, L.Hh, L.zs, L.ssS, L.ssE = s("PV"), s("Dy"), s("Hh"), s("zs"), s("ssS"), s("ssE")
                L.ssX, L.ssN, L.ssT, L.ssP, L.ssO, L.ssY = s("ssX"), s("ssN"), s("ssT"), s("ssP"), s("ssO"), s("ssY")
                L.ssH, L.bout, L.kset = s("ssH"), s("bout"), s("kset")
            if kind == "c":
                L.u0, L.r0 = c.take(2 * KT + 4 + KT, 2 * KT + 16 + KT)

                def result_of(u, L=L):
                    n, t = divmod(u - L.u0 - KT, 3)
                    if n >= 4:
                        return L.r0 + KT + 24 + (u - L.u0 - KT - 12)
                    return L.r0 + KT + 6 * n + (0, 1, 5)[t] if n >= 0 else L.r0 + u - L.u0

                L.result_of = result_of
                L.xc = at(n + "xc", O_AT, [P, KT, NT])
                L.gate = at(n + "gate", O_AT + KT * TILE, [P, KT, NT])
                L.y_hi = at(n + "y_hi", O_AT, [P, KT, NT], F32R)
                L.y_lo = at(n + "y_lo", O_AT + KT * TILE, [P, KT, NT], F32R)
                L.acc = at(n + "acc", H_AT, [P, KT, NT])
                o = X_AT
                L.xc_hi = at(n + "xc_hi", sq_at, [P, 2, NT], F32R)
                L.xr = at(n + "xr", o, [P, CONV - 1 + NT])
                L.xc_lo = [at(n + "xc_lo0", o, [P, NT], F32R), keep(n + "xc_lo1", [P, NT], F32R)]
                o += (CONV - 1 + NT + 5) * 4
                L.st = at(n + "st", o, [P, KT, CONV, NS]); o += KT * CONV * NS * 4
                L.h0 = at(n + "h0", o, [P, KT, NS]); o += KT * NS * 4
                L.cp = at(n + "cp", o, [P, KT, CONV - 1]); o += 96
                L.hp = at(n + "hp", o, [P, KT]); o += 32
                L.hn = at(n + "hn", o, [P, KT, NS]); o += 256
                L.sp = at(n + "sp", o, [P, 6, KT]); o += 192
                o += -o % 32
                L.rt = at(n + "rt", o, [P, 2, NT]); o += 2 * TILE
                L.it = at(n + "it", o, [P, 2, NT]); o += 2 * TILE
                L.rc = at(n + "rc", o, [P, NT]); o += TILE
                L.dn = at(n + "dn", o, [P, NT]); o += TILE
                assert o <= X_AT + KT * TILE
                L.hs = L.dn
                L.c_in, L.sp_e, L.sp_done, L.conv_done, L.g_act, L.xh = s("c_in"), s("sp_e"), s("sp_done"), s("conv_done"), s("g_act"), s("xh")
                L.xsplit, L.sig, L.th, L.root2, L.used, L.y_done = s("xsplit"), s("sig"), s("th"), s("root2"), s("used"), s("y_done")
                L.cout = s("cout")
            layers.append(L)
        assert c.unit == N_UNITS
        final = sem("final")

        STAT = [(5, 504, T, NS), (6, 0, 0, 512), (7, 0, 512, 512)]

        def psum_result(slot):
            return ps[:, 3 * slot:3 * slot + 3, 0:CW]

        def chunks(ap):
            return ap.rearrange("p (c n) -> p c n", c=CH)

        def tile_of(t, m):
            if isinstance(m, int):
                return t[:, m, :]
            return t[:, bass.ds(m, 1), :].rearrange("p o n -> p (o n)")

        def col_of(t, j, m):
            if isinstance(m, int):
                return t[:, j, m:m + 1]
            return t[:, j, bass.ds(m, 1)]

        block = ctx.enter_context(nc.Block())

        @block.sync
        def _(sp):
            for k in range(2):
                sp.dma_start(w_raw[:, k], io["wu"][k].rearrange("p (k m) -> p k m", m=P)).then_inc(w_loaded[k], 16)
            for k in range(KT):
                sp.dma_start(x[:, k, :], io["xt"][k]).then_inc(x_in[k], 16)
            with sp.Fori(1, N_UNITS // 2) as i:
                for j in range(2):
                    sp.wait_ge(w_lo_done, 2 * i + (j - 1))
                    sp.dma_start(w_raw[:, j], io["wu"][bass.ds(2 * i + j, 1)].rearrange("o p (k m) -> p (o k) m", m=P)
                                 ).then_inc(w_loaded[j], 16)

        @block.gpsimd
        def _(pool):
            zeros = zero[:, 0:1].to_broadcast([P, 8 * P])

            def split(j, loaded, n):
                pool.wait_ge(w_loaded[j], loaded)
                nc.gpsimd.tensor_tensor(w_hi[:, j].rearrange("p k m -> p (k m)"), w_raw[:, j].rearrange("p k m -> p (k m)"),
                                        zeros, ALU.add).then_inc(w_hi_done, 1)
                pool.wait_ge(w_hi_done, n + 1)
                nc.gpsimd.tensor_tensor(w_lo[:, j].rearrange("p k m -> p (k m)"), w_raw[:, j].rearrange("p k m -> p (k m)"),
                                        w_hi[:, j].rearrange("p k m -> p (k m)"), ALU.subtract).then_inc(w_lo_done, 1)

            pool.wait_ge(setup, 1)
            for j in range(2):
                split(j, 16, j)
            def refill(first, last, extra):
                with pool.Fori(first // 2, last // 2) as i:
                    for j in range(2):
                        pool.wait_ge(result, 2 * i + (j - 1 + extra))
                        split(j, 16 * i + 16, 2 * i + j)

            def scale(L):
                pool.wait_ge(*L.rp_done.at(1))
                for k in range(1, KT):
                    nc.gpsimd.tensor_tensor(L.acc[:, k, :], L.acc[:, k, :], rx[:], ALU.mult).then_inc(L.scaled.sem, 1)

            def normals(L):
                def quad(p, cq):
                    pool.wait_ge(*L.Rq.at(cq + 1))
                    nc.gpsimd.tensor_tensor(L.sc[:, p], L.sc[:, p],
                                            L.rq[:, p].rearrange("p (h o) -> p h o", o=1).to_broadcast([P, 4, 2 * WIN]),
                                            ALU.mult).then_inc(L.C.sem, 1)

                with pool.Fori(0, 2 * NBLK) as i:
                    for p in range(2):
                        quad(p, 2 * i + p)

            LA, LB, LC, LZ = layers
            refill(2, LB.u0 + 2, 0)
            scale(LA)
            refill(LB.u0 + 2, LB.u0 + 2 * KT + 4, 0)
            normals(LB)
            refill(LB.u0 + 2 * KT + 4, LC.u0 + 2, 0)
            scale(LB)
            refill(LC.u0 + 2, LC.u0 + KT + 4, 0)
            for u in range(LC.u0 + KT + 4, LC.u0 + 2 * KT + 6):
                pool.wait_ge(result, LC.result_of(u - 2) + 1)
                split(u % 2, 16 * (u // 2) + 16, u)
            refill(LC.u0 + 2 * KT + 6, LZ.u0 + 2, 12)
            scale(LC)
            refill(LZ.u0 + 2, N_UNITS, 12)
            scale(LZ)

        @block.tensor
        def _(pe):
            def product(slot, w, slots, hi, lo, tiles, ready=None):
                for n, (k, m) in enumerate(zip(slots, tiles)):
                    if ready is not None:
                        pe.wait_ge(*ready[0].at(ready[1] + n + 1))
                    for t, (wt, mv) in enumerate(((w_hi, hi), (w_hi, lo), (w_lo, hi))):
                        for ch in range(CH):
                            mm = nc.tensor.matmul(ps[:, 3 * slot + ch, 0:CW], wt[:, w, k, :],
                                                  mv[:, m, ch * CW:(ch + 1) * CW],
                                                  start=(n == 0 and t == 0), stop=(n == len(slots) - 1 and t == 2))
                return mm

            def unit(w, slot, u, r, hi, lo, ready=None, tile0=0):
                pe.wait_ge(w_lo_done, u + 1)
                if not (isinstance(r, int) and r < 2):
                    pe.wait_ge(evac[slot], freed(r, slot))
                product(slot, w, range(8), hi, lo, range(tile0, tile0 + 8), ready).then_inc(result, 1)

            def freed(r, slot):
                return r[1] if isinstance(r, tuple) else r // 2

            def units(n, u, r, hi, lo, ready=None, tile0=0):
                for j in range(2):
                    unit((u + j) % 2, (r + j) % 2, u + j, r + j, hi, lo, ready, tile0)
                if n > 2:
                    with pe.Fori(1, n // 2) as i:
                        for j in range(2):
                            unit((u + j) % 2, (r + j) % 2, 2 * i + (u + j), (None, i + (r + j) // 2), hi, lo, None, tile0)

            def column_sums(src, signal):
                for bank, col, tok, n in STAT:
                    mm = nc.tensor.matmul(ps[:, bank, col:col + n], ones[:, :], src[:, tok:tok + n], start=True, stop=True)
                    if bank != 6:
                        mm.then_inc(signal.sem, 1)

            def first_unit(L):
                pe.wait_ge(w_lo_done, L.u0 + 1)
                if L.r0:
                    pe.wait_ge(evac[0], L.r0 // 2)
                for k in range(KT):
                    pe.wait_ge(*L.h_done.at(k + 1))
                    for t, (wt, mv) in enumerate(((w_hi, L.h_hi), (w_hi, L.h_lo), (w_lo, L.h_hi))):
                        for ch in range(CH):
                            mm = nc.tensor.matmul(ps[:, ch, 0:CW], wt[:, 0, k, :], mv[:, k, ch * CW:(ch + 1) * CW],
                                                  start=(k == 0 and t == 0), stop=(k == KT - 1 and t == 2))
                    if k == KT - 1:
                        mm.then_inc(result, 1)
                    pe.wait_ge(*L.sq_done.at(k + 1))
                    for bank, col, tok, n in STAT:
                        mm = nc.tensor.matmul(ps[:, bank, col:col + n], ones[:, :], sq2[:, k % 2, tok:tok + n],
                                              start=(k == 0), stop=(k == KT - 1))
                        if k == KT - 1 and bank != 6:
                            mm.then_inc(L.ssq_mm.sem, 1)
                    if k < KT - 2:
                        mm.then_inc(L.sq_used.sem, 1)
                pe.wait_ge(*L.root.at(1))

            def post(L):
                pe.wait_ge(*L.yssq_done.at(KT))
                column_sums(ssq, L.yssq_mm)
                pe.wait_ge(*L.yroot.at(1))

            def first_units(n, L, hi, lo):
                u, r = L.u0, L.r0
                first_unit(L)
                unit(1, 1, u + 1, r + 1, hi, lo)
                if n > 2:
                    with pe.Fori(1, n // 2) as i:
                        for j in range(2):
                            unit((u + j) % 2, (r + j) % 2, 2 * i + (u + j), (None, i + (r + j) // 2), hi, lo)

            def layer_a(L):
                u, r = L.u0, L.r0
                assert u % 2 == 0 and r % 2 == 0
                first_units(MA, L, L.h_hi, L.h_lo)
                u, r = u + MA, r + MA

                def turn(m):
                    pe.wait_ge(*L.vst.at(m + 1))
                    pe.wait_ge(*L.y_done.at(m)) if not (isinstance(m, int) and m == 0) else pe.wait_ge(*L.stat.at(4))
                    for b in range(NBLK):
                        mm = nc.tensor.transpose(ps[:, 6 + b // 4, (b % 4) * P:(b % 4 + 1) * P],
                                                 L.vstage[:, b * P:(b + 1) * P], ident[:, :])
                    mm.then_inc(L.vT.sem, 1)

                def mixing(m, g):
                    pe.wait_ge(*L.vTl.at(m + 1))
                    for b in range(NBLK):
                        out = ps[:, 6 + b // 4, (b % 4) * P:(b % 4 + 1) * P]
                        for t, (vt, ws) in enumerate(((vt_hi, L.ws_hi), (vt_hi, L.ws_lo), (vt_lo, L.ws_hi))):
                            mm = nc.tensor.matmul(out, vt[:, b, :], ws[:, g, :], start=(t == 0), stop=(t == 2))
                    mm.then_inc(L.mix.sem, 1)

                unit(0, 0, u, r, L.h_hi, L.h_lo)
                pe.wait_ge(*L.vsum_done.at(2 * MA))
                column_sums(L.vsum, L.stat_mm)
                pe.wait_ge(*L.stat.at(1))
                unit(1, 1, u + 1, r + 1, L.h_hi, L.h_lo)
                pe.wait_ge(*L.stat.at(2))
                pe.wait_ge(evac[1], (r + 2) // 2)
                column_sums(ssq, L.stat_mm)

                def body(m, g):
                    even = isinstance(m, int)
                    unit(0, 0, 2 * m + u, r + 2 * m if even else (None, m + r // 2), L.h_hi, L.h_lo)
                    turn(m - 1)
                    unit(1, 1, 2 * m + (u + 1), r + 1 + 2 * m if even else (None, m + r // 2), L.h_hi, L.h_lo)
                    mixing(m - 1, g)

                body(1, 0)
                for g in range(4):
                    with pe.Fori(max(2, 4 * g + 1), min(MA, 4 * g + 5)) as m:
                        body(m, g)
                pe.wait_ge(*L.ws_done.at(1))
                u, r = u + 2 * MA, r + 2 * MA
                unit(0, 0, u, r, L.y_hi, L.y_lo_a, (L.y_lo_done, 0))
                turn(MA - 1)
                unit(1, 1, u + 1, r + 1, L.y_hi, L.y_lo_a)
                mixing(MA - 1, 3)
                with pe.Fori(1, KT // 2) as i:
                    for j in range(2):
                        unit(j, j, 2 * i + (u + j), (None, i + (r + j) // 2), L.y_hi, L.y_lo_a)
                u, r = u + KT, r + KT
                units(KT, u, r, Shift(L.y_hi, KT), L.y_lo_a, (L.y_lo_done, KT))
                post(L)

            class Shift:

                def __init__(self, t, k):
                    self.t, self.k = t, k

                def __getitem__(self, key):
                    a, m, c_ = key
                    return self.t[a, m + self.k, c_]

            def layer_b(L):
                u, r = L.u0, L.r0
                first_unit(L)
                unit(1, 1, u + 1, r + 1, L.h_hi, L.h_lo)
                units(2, u + 2, r + 2, L.h_hi, L.h_lo)
                pe.wait_ge(*L.vf_done.at(1))
                pe.wait_ge(*L.rx_done.at(1))
                for b in range(NBLK):
                    mm = nc.tensor.transpose(ps[:, 6 + b // 4, (b % 4) * P:(b % 4 + 1) * P],
                                             L.vf[:, b * P:(b + 1) * P], ident[:, :])
                mm.then_inc(L.v_tr.sem, 1)
                units(2, u + 4, r + 4, L.h_hi, L.h_lo)
                pe.wait_ge(*L.vtok_done.at(1))
                nc.tensor.transpose(ps[0:2 * NS, 6, 0:P], L.vfs[:, :], ident[:, :]).then_inc(L.v_tr.sem, 1)
                units(2 * KT - 4, u + 6, r + 6, L.h_hi, L.h_lo)
                pe.wait_ge(evac[0], (r + 2 * KT + 2) // 2)
                pe.wait_ge(evac[1], (r + 2 * KT + 2) // 2)
                pe.wait_ge(*L.vtok_done.at(2))

                def scores(n, qd, cq):
                    p, kv = qd % 2, qd // 2
                    pe.wait_ge(*L.stq.at(cq + 1))
                    if not (isinstance(cq, int) and cq < 2):
                        pe.wait_ge(*L.B.at(cq - 1))
                    keys = L.kd[:, kv, n * WIN:(n + 2) * WIN] if isinstance(n, int) else L.kd[:, kv, bass.ds(n * WIN, 2 * WIN)]
                    for h in range(4):
                        mm = nc.tensor.matmul(ps[:, 2 * p + h // 2, (h % 2) * 2 * WIN:(h % 2 + 1) * 2 * WIN],
                                              L.qs[:, p, h, :], keys, start=True, stop=True)
                    mm.then_inc(L.S.sem, 1)

                def turns(qd, cq):
                    p = qd % 2
                    pe.wait_ge(*L.C.at(cq + 1))
                    if not (isinstance(cq, int) and cq < 1):
                        pe.wait_ge(*L.PC.at(cq))
                    for h in range(4):
                        for sb_ in range(2):
                            mm = nc.tensor.transpose(ps[:, 4 + sb_, h * P:(h + 1) * P],
                                                     L.sc[:, p, h, sb_ * WIN:(sb_ + 1) * WIN], ident[:, :])
                    mm.then_inc(L.TP.sem, 1)

                def values(qd, cq):
                    p = qd % 2
                    pe.wait_ge(*L.PC.at(cq + 1))
                    pe.wait_ge(*L.stv.at(cq + 1))
                    if not (isinstance(cq, int) and cq < 2):
                        pe.wait_ge(*L.Dy.at(cq - 1))
                    for sb_ in range(2):
                        mm = nc.tensor.matmul(ps[:, 6 + p, :], L.vs[:, p, sb_, :], L.pt[:, p, sb_, :],
                                              start=(sb_ == 0), stop=(sb_ == 1))
                    mm.then_inc(L.PV.sem, 1)

                def block_step(n, first=False, last=False):
                    for qd in range(4):
                        cq = 4 * n + qd
                        if not (last and qd >= 2):
                            scores(n + (qd + 2) // 4, (qd + 2) % 4, cq + 2)
                        if not (first and qd == 0):
                            values((qd + 3) % 4, cq - 1)
                        turns(qd, cq)

                scores(0, 0, 0)
                scores(0, 1, 1)
                block_step(0, first=True)
                with pe.Fori(1, NBLK - 1) as n:
                    block_step(n)
                block_step(NBLK - 1, last=True)
                values(3, 4 * NBLK - 1)
                pe.wait_ge(*L.zs.at(1))
                pe.wait_ge(*L.PC.at(4 * NBLK))
                pe.wait_ge(*L.B.at(4 * NBLK))
                for e in range(2 * NS):
                    b, kv = e // 2, e % 2
                    mm = nc.tensor.matmul(ps[0:8, e // 3, (e % 3) * (WIN + 1):(e % 3 + 1) * (WIN + 1)],
                                          L.qz[:, b, 8 * kv:8 * kv + 8], L.kc[:, kv, b, :], start=True, stop=True)
                mm.then_inc(L.ssS.sem, 1)
                pe.wait_ge(*L.ssN.at(1))
                pe.wait_ge(*L.Dy.at(4 * NBLK))
                for e in range(2 * NS):
                    nc.tensor.transpose(ps[:, 6, e * 8:(e + 1) * 8], L.ss[0:8, e, 0:WIN], ident[0:8, 0:8])
                nc.tensor.transpose(ps[0:2 * NS, 7, 0:8], L.ss[0:8, :, WIN], ident[0:8, 0:8]).then_inc(L.ssT.sem, 1)
                pe.wait_ge(*L.ssP.at(1))
                nc.tensor.matmul(ps[:, 0, 0:P], L.v16[0:2 * NS, :], L.zo[0:2 * NS].rearrange("p a b -> p (a b)"),
                                 start=True, stop=False)
                for b in range(NS):
                    mm = nc.tensor.matmul(ps[:, 0, b * 16:(b + 1) * 16], L.vc[:, b, :], L.pts[:, b * 16:(b + 1) * 16],
                                          start=False, stop=(b == NS - 1))
                mm.then_inc(L.ssO.sem, 1)
                pe.wait_ge(*L.y_lo_done.at(1))
                units(KT, u + 2 * KT + 2, r + 2 * KT + 2, L.y_hi, L.y_lo, None)
                post(L)

            def layer_c(L):
                u, r = L.u0, L.r0
                first_units(KT, L, L.h_hi, L.h_lo)
                for n in range(4):
                    for t in range(2):
                        u_ = u + KT + 3 * n + t
                        unit(u_ % 2, t, u_, L.result_of(u_), L.h_hi, L.h_lo)
                    u_ = u + KT + 3 * n + 2
                    first = L.result_of(u_) - 3
                    pe.wait_ge(w_lo_done, u_ + 1)
                    pe.wait_ge(*L.xsplit.at(2 * n + 2))
                    for q in range(4):
                        pe.wait_ge(evac[q % 2], (first + q) // 2)
                        for i in range(2):
                            for t, (wt, mv) in enumerate(((w_hi, L.xc_hi[:, i]), (w_hi, L.xc_lo[i]), (w_lo, L.xc_hi[:, i]))):
                                for ch in range(CH):
                                    mm = nc.tensor.matmul(ps[:, 3 * (q % 2) + ch, 0:CW], wt[:, u_ % 2, 2 * q + i, :],
                                                          mv[:, ch * CW:(ch + 1) * CW],
                                                          start=(i == 0 and t == 0), stop=(i == 1 and t == 2))
                        mm.then_inc(result, 1)
                units(KT, u + KT + 12, r + KT + 24, L.y_hi, L.y_lo, (L.y_lo_done, 0))
                post(L)

            pe.wait_ge(setup, 1)
            pe.wait_ge(consts, 16 * n_consts)
            for L in layers:
                if L.kind == "a":
                    L.y_lo_a = L.y_lo
                    layer_a(L)
                elif L.kind == "b":
                    layer_b(L)
                else:
                    layer_c(L)

        @block.scalar
        def _(act):
            act.dma_start(ident[:, :], io["ident"]).then_inc(consts, 16)
            act.dma_start(g_pre[:], io["g_pre"]).then_inc(consts, 16)
            act.dma_start(g_post[:], io["g_post"]).then_inc(consts, 16)
            act.dma_start(ln_g[:], io["ln_g"]).then_inc(consts, 16)
            act.dma_start(ln_b[:], io["ln_b"]).then_inc(consts, 16)
            act.dma_start(cvec[:], io["cvec"]).then_inc(consts, 16)

            def pre(L, prev):
                if L.i == 0:
                    act.wait_ge(consts, 16 * n_consts)
                    act.wait_ge(setup, 1)
                for k in range(KT):
                    if prev is None:
                        act.wait_ge(x_in[k], 16)
                    else:
                        act.wait_ge(*prev.x_new.at(k + 1))
                    nc.scalar.activation(L.h_hi[:, k, :], x[:, k, :], ACT.Copy, scale=g_pre[:, L.i, k:k + 1]
                                         ).then_inc(L.hi_done.sem, 1)
                    if k >= 2:
                        act.wait_ge(*L.sq_used.at(k - 1))
                    nc.scalar.activation(sq2[:, k % 2, :], x[:, k, :], ACT.Square).then_inc(L.sq_done.sem, 1)
                    act.dma_start(io["x_save"][k], x[:, k, :]).then_inc(L.x_saved.sem, 16)
                root(L.root, L.ssq_mm)

            def settle():
                nc.scalar.activation(cell_act[0:1, 0:1], zero[0:1, 0:1], ACT.Copy)
                nc.scalar.drain()

            def read_sums(dst, signal, mm, func, **how):
                act.wait_ge(*mm.at(1))
                nc.scalar.activation(dst[:, T:NT], ps[:, 5, 504:512], func, **how)
                nc.scalar.drain().then_inc(signal.sem, 1)
                act.wait_ge(*mm.at(2))
                nc.scalar.activation(dst[:, 0:T].rearrange("p (a b) -> p a b", a=2), ps[:, 6:8, :], func, **how)
                nc.scalar.drain().then_inc(signal.sem, 1)

            def root(signal, mm):
                read_sums(rx, signal, mm, ACT.Sqrt, scale=1.0 / D, bias=eps[:, 0:1])

            def x_back(L):
                for k in range(KT):
                    act.dma_start(x[:, k, :], io["x_save"][k]).then_inc(L.x_back.sem, 16)

            def out_single(L, r):
                for m in range(KT):
                    act.wait_ge(result, r + m + 1)
                    nc.scalar.activation(chunks(L.acc[:, m, :]), psum_result((r + m) % 2), ACT.Copy)
                    nc.scalar.drain().then_inc(evac[(r + m) % 2], 1)
                    act.wait_ge(*L.yssq_done.at(m)) if m else None
                    nc.scalar.activation(sqt[:], L.acc[:, m, :], ACT.Square).then_inc(L.ysq_done.sem, 1)
                root(L.yroot, L.yssq_mm)

            def layer_a(L):
                act.wait_ge(*L.x_saved.at(16 * KT))
                act.wait_ge(*L.h_done.at(KT))
                act.dma_start(L.wsr[:], io["wst"][L.j]).then_inc(L.ws_in.sem, 16)
                act.dma_start(L.tri[:], io["tri"]).then_inc(L.ws_in.sem, 16)
                act.dma_start(bs_bc[:], io["bs"][L.j:L.j + 1].partition_broadcast(P).rearrange("p o g t -> p (o g) t")
                              ).then_inc(L.ws_in.sem, 16)
                act.dma_start(corner[:], io["corner"][L.j:L.j + 1].partition_broadcast(P).rearrange("p o g -> p (o g)")
                              ).then_inc(L.ws_in.sem, 16)
                act.wait_ge(*L.wm.at(1))
                nc.scalar.activation(L.ws_hi[:], L.wsr[:], ACT.Copy).then_inc(L.wh.sem, 1)

                def gelu_v(m, j):
                    act.wait_ge(*L.in_done.at(m + 1))
                    settle()
                    nc.scalar.activation(tile_of(L.v, m), L.tmp[:, j, :], ACT.Gelu_apprx_tanh)
                    nc.scalar.drain().then_inc(L.act_done.sem, 1)
                    if not (isinstance(m, int) and m == 0):
                        act.wait_ge(*L.vsum_done.at(2 * m))
                    settle()
                    nc.scalar.activation(sqt[:], tile_of(L.v, m), ACT.Square).then_inc(L.vsq.sem, 1)

                for j in range(2):
                    gelu_v(j, j)
                with act.Fori(1, MA // 2) as i:
                    for j in range(2):
                        gelu_v(2 * i + j, j)

                def gates(m):
                    act.wait_ge(*L.in_done.at(2 * m + (MA + 1)))
                    nc.scalar.activation(L.tmp[:, 0, :], L.tmp[:, 0, :], ACT.Gelu_apprx_tanh).then_inc(L.u_act.sem, 1)

                def silu(m):
                    act.wait_ge(*L.in_done.at(2 * m + (MA + 2)))
                    nc.scalar.activation(L.tmp[:, 1, :], L.tmp[:, 1, :], ACT.Silu).then_inc(L.g_act.sem, 1)

                def high(m):
                    act.wait_ge(*L.vT.at(m + 1))
                    nc.scalar.activation(vt_hi[:].rearrange("p (a b) n -> p a (b n)", a=2), ps[:, 6:8, :], ACT.Copy
                                         ).then_inc(L.vTh.sem, 1)

                gates(0)
                read_sums(L.mu, L.stat, L.stat_mm, ACT.Copy, scale=1.0 / DA)
                silu(0)
                read_sums(L.rstd, L.stat, Signal(L.stat_mm.sem, L.stat_mm.base + 2), ACT.Copy, scale=1.0 / DA)
                act.wait_ge(*L.var_done.at(1))
                nc.scalar.activation(L.rstd[:], L.rstd[:], ACT.Sqrt, bias=eps[:, 1:2]).then_inc(L.stat.sem, 1)

                def body(m):
                    gates(m)
                    high(m - 1)
                    silu(m)

                body(1)
                with act.Fori(2, MA) as m:
                    body(m)
                r = L.r0 + 3 * MA

                def split(m):
                    act.wait_ge(*L.y_done.at(m + 1))
                    if m >= 2:
                        act.wait_ge(*L.lo_cut.at(m - 1))
                    nc.scalar.activation(L.y_tmp[:, m % 2, :], L.y[:, m, :], ACT.Copy).then_inc(L.tmp_hi.sem, 1)

                def in_place(m):
                    act.wait_ge(*L.lo_cut.at(m + 1))
                    nc.scalar.activation(L.y_hi[:, m, :], L.y[:, m, :], ACT.Copy).then_inc(L.y_lo_done.sem, 1)

                def split_all(m0):
                    split(m0)
                    for m in range(m0, m0 + KT):
                        if m + 1 < m0 + KT:
                            split(m + 1)
                        in_place(m)

                act.wait_ge(result, L.r0 + 3 * MA)
                act.wait_ge(*L.y_done.at(MA - 1))
                act.wait_ge(*L.vst.at(MA))
                split_all(0)
                high(MA - 1)
                for m in range(KT):
                    act.wait_ge(result, r + m + 1)
                    nc.scalar.activation(chunks(L.acc[:, m, :]), psum_result(m % 2), ACT.Copy)
                    nc.scalar.drain().then_inc(evac[m % 2], 1)
                act.wait_ge(result, L.r0 + 3 * MA + KT)
                split_all(KT)
                x_back(L)
                for m in range(KT):
                    act.wait_ge(*L.acc_done.at(m + 1))
                    act.wait_ge(*L.yssq_done.at(m)) if m else None
                    nc.scalar.activation(sqt[:], L.acc[:, m, :], ACT.Square).then_inc(L.ysq_done.sem, 1)
                root(L.yroot, L.yssq_mm)

            def layer_b(L):
                act.wait_ge(*L.x_saved.at(16 * KT))
                act.wait_ge(*L.h_done.at(KT))
                act.dma_start(L.cos[:], io["cos"]).then_inc(L.rope_in.sem, 16)
                act.dma_start(L.sin[:], io["sin"]).then_inc(L.rope_in.sem, 16)
                act.dma_start(L.sink[:], io["sink"].partition_broadcast(P).rearrange("p o h -> p (o h)")).then_inc(L.rope_in.sem, 16)

                def swap(src):
                    for a in range(4):
                        b = a ^ 1
                        rows, other = slice(32 * a, 32 * a + 32), slice(32 * b, 32 * b + 32)
                        act.dma_start(L.sw[rows, :], src(other)).then_inc(L.sw_done.sem, 16)

                act.wait_ge(*L.in_done.at(1))
                swap(lambda rows: L.kf[rows, :])
                act.wait_ge(*L.k_rot.at(1))
                for kv in range(2):
                    for half in range(2):
                        nc.scalar.activation(L.kd[64 * half:64 * half + 64, kv, P:P + NT], L.kf[64 * kv:64 * kv + 64, :], ACT.Copy)
                nc.scalar.drain().then_inc(L.kset.sem, 1)
                act.dma_start(io["kp"], L.kf[:, T - WIN:T]).then_inc(L.kout.sem, 16)
                act.dma_start(io["ks"][:, WIN - 1, :], L.kf[:, T:NT]).then_inc(L.kout.sem, 16)
                act.dma_start(io["ks"][:, 0:WIN - 1, :], io["kct"][:, 1:WIN, :]).then_inc(L.kout.sem, 16)
                act.dma_start(io["vs"][:, 0:WIN - 1, :], io["vct"][:, 1:WIN, :]).then_inc(L.kout.sem, 16)
                def q_swap(m):
                    act.wait_ge(*L.in_done.at(m + 3))
                    for a in range(4):
                        b = a ^ 1
                        rows = slice(32 * b, 32 * b + 32)
                        src = L.q[rows, m, :] if isinstance(m, int) else L.q[rows, bass.ds(m, 1), :].rearrange("p o n -> p (o n)")
                        act.dma_start(L.sw[32 * a:32 * a + 32, :], src).then_inc(L.sw_done.sem, 16)

                with act.Fori(0, KT) as m:
                    q_swap(m)
                with act.Fori(0, KT) as m:
                    act.wait_ge(*L.in_done.at(m + (KT + 3)))
                    settle()
                    nc.scalar.activation(tile_of(L.gate, m), L.sw[:], ACT.Silu).then_inc(L.act_done.sem, 1)
                act.wait_ge(result, L.r0 + 2 * KT + 2)
                act.dma_start(L.mask[:], io["mask"]).then_inc(L.at_in.sem, 16)
                act.dma_start(L.kc[:, :, :, 0:WIN], io["kcd"]).then_inc(L.at_in.sem, 16)
                act.dma_start(L.vc[:], io["vct"].rearrange("b s f -> s b f")).then_inc(L.at_in.sem, 16)
                act.dma_start(L.sk[0:8, :], io["sink8"]).then_inc(L.at_in.sem, 16)
                act.dma_start(L.dx[0:16], io["dx"]).then_inc(L.at_in.sem, 16)
                act.wait_ge(*L.vtok_done.at(2))
                act.dma_start(io["vp"], L.vtok[:, NBLK, :]).then_inc(L.kout.sem, 16)
                act.dma_start(io["vs"][:, WIN - 1, :], L.v16[0:16:2, :]).then_inc(L.kout.sem, 16)

                def exps(qd, cq):
                    p = qd % 2
                    act.wait_ge(*L.B.at(cq + 1))
                    for h in range(4):
                        nc.scalar.activation(L.sc[:, p, h, :], L.sc[:, p, h, :], ACT.Exp, bias=L.mx[:, p, 1, h:h + 1],
                                             accum_out=L.mx[:, p, 2, h:h + 1])
                    nc.scalar.activation(L.mx[:, p, 3, :], L.mx[:, p, 3, :], ACT.Exp)
                    nc.scalar.drain().then_inc(L.X.sem, 1)

                def copies(qd, cq):
                    p = qd % 2
                    act.wait_ge(*L.TP.at(cq + 1))
                    if not (isinstance(cq, int) and cq < 2):
                        act.wait_ge(*L.PV.at(cq - 1))
                    nc.scalar.activation(L.pt[:, p], ps[:, 4:6, :], ACT.Copy).then_inc(L.PC.sem, 1)

                def highs(n, qd, cq):
                    p = qd % 2
                    act.wait_ge(*L.Dy.at(cq + 1))
                    settle()
                    nc.scalar.activation(L.y_hi[:, 2 * qd:2 * qd + 2, bass.ds(n * WIN, WIN) if not isinstance(n, int) else slice(n * WIN, n * WIN + WIN)],
                                         L.yt[:, p], ACT.Copy).then_inc(L.Hh.sem, 1)

                def block_step(n, first=False, last=False):
                    for qd in range(4):
                        cq = 4 * n + qd
                        if not (last and qd == 3):
                            exps((qd + 1) % 4, cq + 1)
                        if not (first and qd == 0):
                            highs(n if qd else n - 1, (qd + 3) % 4, cq - 1)
                        copies(qd, cq)

                exps(0, 0)
                block_step(0, first=True)
                with act.Fori(1, NBLK - 1) as n:
                    block_step(n)
                block_step(NBLK - 1, last=True)
                highs(NBLK - 1, 3, 4 * NBLK - 1)
                act.wait_ge(*L.ssE.at(1))
                nc.scalar.activation(L.ss[0:8], L.ss[0:8], ACT.Exp)
                nc.scalar.activation(L.sm[0:8, 2], L.sm[0:8, 2], ACT.Exp)
                nc.scalar.drain().then_inc(L.ssX.sem, 1)
                act.wait_ge(*L.ssY.at(1))
                nc.scalar.activation(L.y_hi[:, :, T:NT], L.ys[:], ACT.Copy).then_inc(L.ssH.sem, 1)
                act.wait_ge(*L.kout.at(16 * 6))
                x_back(L)
                act.wait_ge(*L.Hh.at(4 * NBLK))
                out_single(L, L.r0 + 2 * KT + 2)

            def layer_c(L):
                act.wait_ge(*L.x_saved.at(16 * KT))
                act.wait_ge(*L.h_done.at(KT))
                act.dma_start(L.st[:, :, 0:CONV - 1, :], io["st"]).then_inc(L.c_in.sem, 16)
                act.dma_start(L.h0[:], io["h0"]).then_inc(L.c_in.sem, 16)
                act.wait_ge(consts, 16 * n_consts)
                nc.scalar.activation(L.sp[:, 0], cvec[:, 7], ACT.Abs)
                nc.scalar.drain()
                nc.scalar.activation(L.sp[:, 0], L.sp[:, 0], ACT.Exp, scale=-1.0).then_inc(L.sp_e.sem, 1)
                act.wait_ge(*L.sp_done.at(1))

                def y_high(m):
                    act.wait_ge(*L.y_done.at(m + 1))
                    nc.scalar.activation(L.y_hi[:, m, :], L.hs[:], ACT.Copy).then_inc(L.y_hi_done.sem, 1)

                def square_root(m):
                    nc.scalar.activation(L.rc[:], L.rt[:, m % 2, :], ACT.Sqrt).then_inc(L.root2.sem, 1)

                def silu(m):
                    act.wait_ge(*L.in_done.at(m + 1))
                    nc.scalar.activation(L.gate[:, m, :], L.gate[:, m, :], ACT.Silu).then_inc(L.g_act.sem, 1)

                act.wait_ge(*L.conv_done.at(1))
                for n in range(4):
                    if n:
                        act.wait_ge(result, L.result_of(L.u0 + KT + 3 * n - 1) + 1)
                    for t in range(2):
                        nc.scalar.activation(L.xc_hi[:, t, :], L.xc[:, 2 * n + t, :], ACT.Copy).then_inc(L.xh.sem, 1)
                    if n:
                        y_high(2 * n - 2)
                        square_root(2 * n - 1)
                    silu(2 * n)
                    if n:
                        y_high(2 * n - 1)
                    silu(2 * n + 1)
                    first = L.result_of(L.u0 + KT + 3 * n + 2) - 3
                    for t in range(2):
                        m = 2 * n + t
                        if n:
                            act.wait_ge(*L.used.at(m - 1))
                        for q, (dst, vec) in enumerate(((L.rt, 5), (L.it, 6))):
                            act.wait_ge(result, first + 2 * t + q + 1)
                            nc.scalar.activation(chunks(dst[:, t, :]), psum_result(q), ACT.Sigmoid, bias=cvec[:, vec, m:m + 1])
                            nc.scalar.drain().then_inc(evac[q], 1)
                        nc.scalar.activation(L.rt[:, t, :], L.rt[:, t, :], ACT.Tanh, scale=L.sp[:, 1, m:m + 1])
                        nc.scalar.drain().then_inc(L.th.sem, 1)
                    square_root(2 * n)
                y_high(2 * KT // 2 - 2)
                square_root(KT - 1)
                y_high(KT - 1)
                act.wait_ge(*L.y_lo_done.at(KT))
                act.dma_start(io["ccp"], L.cp[:]).then_inc(L.cout.sem, 16)
                act.dma_start(io["chp"], L.hp[:]).then_inc(L.cout.sem, 16)
                act.dma_start(io["ccs"], L.st[:, :, 1:CONV, :]).then_inc(L.cout.sem, 16)
                act.dma_start(io["chs"], L.hn[:]).then_inc(L.cout.sem, 16)
                act.wait_ge(*L.cout.at(64))
                x_back(L)
                out_single(L, L.r0 + KT + 24)

            prev = None
            for L in layers:
                pre(L, prev)
                (layer_a if L.kind == "a" else layer_b if L.kind == "b" else layer_c)(L)
                if L.kind == "a":
                    act.dma_start(io["av"][L.j], v_new[:]).then_inc(L.vout.sem, 16)
                    act.wait_ge(*L.vout.at(16))
                prev = L
            for k in range(KT):
                act.wait_ge(*prev.x_new.at(k + 1))
                act.dma_start(io["y"][k], x[:, k, :]).then_inc(final, 16)
            act.wait_ge(final, 16 * KT)

        @block.vector
        def _(dve):
            V = nc.vector
            V.memset(zero[:], 0.0)
            V.memset(ones[:], 1.0)
            V.memset(eps[:, 0:1], 1e-6)
            V.memset(eps[:, 1:2], 1e-5)
            V.drain().then_inc(setup, 1)
            dve.wait_ge(consts, 16 * n_consts)

            def pre(L, prev):
                for k in range(KT):
                    if prev is not None:
                        new_x(prev, k)
                    dve.wait_ge(*L.hi_done.at(k + 1))
                    V.scalar_tensor_tensor(L.h_lo[:, k, :], x[:, k, :], g_pre[:, L.i, k:k + 1], L.h_hi[:, k, :],
                                           ALU.mult, ALU.subtract).then_inc(L.h_done.sem, 1)
                dve.wait_ge(*L.root.at(2))
                V.reciprocal(rx[:], rx[:])
                V.drain().then_inc(L.rx_done.sem, 1)

            def settle():
                V.memset(cell_dve[0:1, 0:1], 0.0)
                V.drain()

            def add_up(total, part, first):
                if first:
                    V.tensor_copy(total[:], part)
                else:
                    V.tensor_tensor(total[:], total[:], part, ALU.add)

            def new_x(L, k):
                if k == 0:
                    dve.wait_ge(*L.yroot.at(2))
                    V.reciprocal(rx[:], rx[:])
                    V.drain().then_inc(L.rp_done.sem, 1)
                    V.tensor_tensor(L.acc[:, k, :], L.acc[:, k, :], rx[:], ALU.mult)
                    V.drain()
                    dve.wait_ge(*L.x_back.at(16 * KT))
                else:
                    dve.wait_ge(*L.scaled.at(k))
                V.scalar_tensor_tensor(x[:, k, :], L.acc[:, k, :], g_post[:, L.i, k:k + 1], x[:, k, :], ALU.mult, ALU.add)
                V.drain().then_inc(L.x_new.sem, 1)

            def read(out, slot, r):
                dve.wait_ge(result, r)
                V.tensor_tensor(chunks(out), psum_result(slot), chunks(rx[:]), ALU.mult)
                V.drain().then_inc(evac[slot], 1)

            def yssq(L):
                for m in range(KT):
                    dve.wait_ge(*L.ysq_done.at(m + 1))
                    add_up(ssq, sqt[:], m == 0)
                    V.drain().then_inc(L.yssq_done.sem, 1)

            def layer_a(L):
                r = L.r0
                dve.wait_ge(*L.ws_in.at(64))
                for g in range(4):
                    V.tensor_tensor(L.wsr[:, g], L.wsr[:, g], L.tri[:], ALU.mult)
                V.drain().then_inc(L.wm.sem, 1)
                dve.wait_ge(*L.wh.at(1))
                V.tensor_tensor(L.ws_lo[:], L.wsr[:], L.ws_hi[:], ALU.subtract).then_inc(L.ws_done.sem, 1)

                def read_v(m, j):
                    read(L.tmp[:, j, :], j, m + (r + 1))
                    V.drain().then_inc(L.in_done.sem, 1)
                    dve.wait_ge(*L.act_done.at(m + 1))
                    add_up(L.vsum, tile_of(L.v, m), isinstance(m, int) and m == 0)
                    V.drain().then_inc(L.vsum_done.sem, 1)
                    dve.wait_ge(*L.vsq.at(m + 1))
                    add_up(ssq, sqt[:], isinstance(m, int) and m == 0)
                    V.drain().then_inc(L.vsum_done.sem, 1)

                for j in range(2):
                    read_v(j, j)
                with dve.Fori(1, MA // 2) as i:
                    for j in range(2):
                        read_v(2 * i + j, j)
                r += MA

                def read_u(m):
                    read(L.tmp[:, 0, :], 0, 2 * m + (r + 1))
                    V.drain().then_inc(L.in_done.sem, 1)

                def read_g(m):
                    read(L.tmp[:, 1, :], 1, 2 * m + (r + 2))
                    V.drain().then_inc(L.in_done.sem, 1)

                def gated(m):
                    dve.wait_ge(*L.u_act.at(m + 1))
                    dve.wait_ge(*L.g_act.at(m + 1))
                    V.tensor_tensor(L.ug[:], L.tmp[:, 0, :], L.tmp[:, 1, :], ALU.mult)
                    V.drain()

                def normal(m):
                    V.tensor_tensor(L.vstage[:], tile_of(L.v, m), L.mu[:], ALU.subtract)
                    V.drain()
                    V.tensor_tensor(L.vstage[:], L.vstage[:], L.rstd[:], ALU.mult)
                    V.drain()
                    V.tensor_scalar(L.vstage[:], L.vstage[:], col_of(ln_g, L.j, m), col_of(ln_b, L.j, m), ALU.mult, ALU.add)
                    V.drain().then_inc(L.vst.sem, 1)
                    V.tensor_copy(tile_of(v_new, m), L.vstage[:, T:NT])

                def low(m):
                    dve.wait_ge(*L.vTh.at(m + 1))
                    V.tensor_tensor(vt_lo[:].rearrange("p (a b) n -> p a (b n)", a=2), ps[:, 6:8, :],
                                    vt_hi[:].rearrange("p (a b) n -> p a (b n)", a=2), ALU.subtract).then_inc(L.vTl.sem, 1)

                def mixed(m, g):
                    yt = tile_of(L.y, m)
                    dve.wait_ge(*L.mix.at(m + 1))
                    V.tensor_tensor(yt[:, 0:T].rearrange("p (a b) -> p a b", b=P),
                                    ps[:, 6:8, :].rearrange("p a (b n) -> p (a b) n", n=P),
                                    bs_bc[:, g:g + 1, :].to_broadcast([P, NBLK, P]), ALU.add)
                    V.tensor_scalar(yt[:, T:NT], L.vstage[:, T:NT], corner[:, g:g + 1], bs_bc[:, g, 0:1], ALU.mult, ALU.add)
                    V.drain()
                    V.tensor_tensor(yt, yt, L.ug[:], ALU.mult)
                    V.drain().then_inc(L.y_done.sem, 1)

                read_u(0)
                read_g(0)
                dve.wait_ge(*L.stat.at(4))
                V.tensor_tensor(L.vstage[:], L.mu[:], L.mu[:], ALU.mult)
                V.drain()
                V.tensor_tensor(L.rstd[:], L.rstd[:], L.vstage[:], ALU.subtract)
                V.drain()
                V.tensor_scalar(L.rstd[:], L.rstd[:], 0.0, None, ALU.max)
                V.drain().then_inc(L.var_done.sem, 1)
                dve.wait_ge(*L.stat.at(5))
                V.reciprocal(L.rstd[:], L.rstd[:])
                V.drain()
                gated(0)

                def body(m, g):
                    normal(m - 1)
                    read_u(m)
                    low(m - 1)
                    read_g(m)
                    mixed(m - 1, g)
                    gated(m)

                body(1, 0)
                for g in range(4):
                    with dve.Fori(max(2, 4 * g + 1), min(MA, 4 * g + 5)) as m:
                        body(m, g)
                normal(MA - 1)

                def cut(m):
                    dve.wait_ge(*L.tmp_hi.at(m + 1))
                    V.tensor_tensor(L.y_lo[:, m % KT, :], L.y[:, m, :], L.y_tmp[:, m % 2, :], ALU.subtract
                                    ).then_inc(L.lo_cut.sem, 1)

                for m in range(KT):
                    cut(m)
                low(MA - 1)
                mixed(MA - 1, 3)
                for m in range(KT, 2 * KT):
                    cut(m)
                r += 2 * MA + KT
                for m in range(KT):
                    dve.wait_ge(result, r + m + 1)
                    V.tensor_tensor(chunks(L.acc[:, m, :]), psum_result(m % 2), chunks(L.acc[:, m, :]), ALU.add)
                    V.drain().then_inc(evac[m % 2], 1)
                    V.drain().then_inc(L.acc_done.sem, 1)
                    dve.wait_ge(*L.ysq_done.at(m + 1))
                    add_up(ssq, sqt[:], m == 0)
                    V.drain().then_inc(L.yssq_done.sem, 1)

            def layer_b(L):
                r = L.r0
                dve.wait_ge(*L.rope_in.at(48))

                def rotate(t, n):
                    dve.wait_ge(*L.sw_done.at(n))
                    V.tensor_tensor(L.sw[:], L.sw[:], L.sin[:], ALU.mult)
                    V.tensor_tensor(t, t, L.cos[:], ALU.mult)
                    V.drain()
                    V.tensor_tensor(t, t, L.sw[:], ALU.add)
                    V.drain()

                read(L.kf[:], 0, r + 1)
                V.drain().then_inc(L.in_done.sem, 1)
                V.memset(L.kd[:, :, 0:P], 0.0)
                V.memset(L.vtok[:, 0, :], 0.0)
                rotate(L.kf[:], 64)
                V.drain().then_inc(L.k_rot.sem, 1)
                read(L.vf[:], 1, r + 2)
                V.tensor_copy(L.vfs[:].rearrange("p (b k) -> p b k", k=2),
                              L.vf[:, T:NT].rearrange("p (b o) -> p b o", o=1).to_broadcast([P, NS, 2]))
                V.drain().then_inc(L.vf_done.sem, 1)
                V.drain().then_inc(L.in_done.sem, 1)
                dve.wait_ge(*L.kset.at(1))

                def read_q(m, slot):
                    read(tile_of(L.q, m), slot, m + (r + 3))
                    V.drain().then_inc(L.in_done.sem, 1)
                    rotate(tile_of(L.q, m), 64 * m + 128)

                for m in range(2):
                    read_q(m, m)
                dve.wait_ge(*L.v_tr.at(1))
                V.tensor_copy(L.vtok[:, 1:NBLK + 1, :], ps[:, 6:8, :].rearrange("p a (b n) -> p (a b) n", n=P))
                V.drain().then_inc(L.vtok_done.sem, 1)
                for m in range(2, 4):
                    read_q(m, m % 2)
                dve.wait_ge(*L.v_tr.at(2))
                V.tensor_copy(L.v16[0:2 * NS, :], ps[0:2 * NS, 6, 0:P])
                V.drain().then_inc(L.vtok_done.sem, 1)
                with dve.Fori(2, KT // 2) as i:
                    for j in range(2):
                        read_q(2 * i + j, j)
                with dve.Fori(0, KT // 2) as i:
                    for j in range(2):
                        read(L.sw[:], j, 2 * i + (r + KT + 3 + j))
                        V.drain().then_inc(L.in_done.sem, 1)
                        dve.wait_ge(*L.act_done.at(2 * i + (j + 1)))
                dve.wait_ge(result, L.r0 + 2 * KT + 2)
                dve.wait_ge(*L.at_in.at(80))

                def cols(n):
                    return slice(n * WIN, (n + 1) * WIN) if isinstance(n, int) else bass.ds(n * WIN, WIN)

                def stage_q(n, qd, cq):
                    p = qd % 2
                    if not (isinstance(cq, int) and cq < 2):
                        dve.wait_ge(*L.S.at(cq - 1))
                    settle()
                    for half in range(2):
                        rows = slice(HD * half, HD * half + HD)
                        V.tensor_copy(L.qs[rows, p, half::2, :], L.q[rows, 2 * qd:2 * qd + 2, cols(n)])
                    V.drain().then_inc(L.stq.sem, 1)

                def stage_v(n, qd, cq):
                    p = qd % 2
                    if not (isinstance(cq, int) and cq < 2):
                        dve.wait_ge(*L.PV.at(cq - 1))
                    settle()
                    src = L.vtok[:, n:n + 2, :] if isinstance(n, int) else L.vtok[:, bass.ds(n, 2), :]
                    V.tensor_copy(L.vs[:, p], src).then_inc(L.stv.sem, 1)

                def maxima(n, qd, cq):
                    p = qd % 2
                    dve.wait_ge(*L.S.at(cq + 1))
                    if not (isinstance(cq, int) and cq < 2):
                        dve.wait_ge(*L.TP.at(cq - 1))
                    settle()
                    which = 0 if (isinstance(n, int) and n == 0) else 1
                    for h in range(4):
                        V.tensor_tensor_reduce(L.sc[:, p, h, :],
                                               ps[:, 2 * p + h // 2, (h % 2) * 2 * WIN:(h % 2 + 1) * 2 * WIN],
                                               L.mask[:, which, :], SCALE, L.sink[:, 4 * qd + h:4 * qd + h + 1],
                                               ALU.add, ALU.max, L.mx[:, p, 0, h:h + 1])
                    V.drain()
                    V.tensor_scalar(L.mx[:, p, 1, :], L.mx[:, p, 0, :], -1.0, None, ALU.mult)
                    V.tensor_tensor(L.mx[:, p, 3, :], L.sink[:, 4 * qd:4 * qd + 4], L.mx[:, p, 0, :], ALU.subtract)
                    V.drain().then_inc(L.B.sem, 1)

                def normals(qd, cq):
                    p = qd % 2
                    dve.wait_ge(*L.X.at(cq + 1))
                    V.tensor_tensor(L.rq[:, p], L.mx[:, p, 2, :], L.mx[:, p, 3, :], ALU.add)
                    V.drain()
                    V.reciprocal(L.rq[:, p], L.rq[:, p])
                    V.drain().then_inc(L.Rq.sem, 1)

                def outputs(n, qd, cq):
                    p, kv = qd % 2, qd // 2
                    dve.wait_ge(*L.PV.at(cq + 1))
                    src = ps[HD * kv:HD * kv + HD, 6 + p, :].rearrange("p (t r n) -> p t r n", t=2, r=2)
                    for half in range(2):
                        rows = slice(HD * half, HD * half + HD)
                        V.tensor_tensor(L.yt[rows, p], src[:, :, half, :], L.gate[rows, 2 * qd:2 * qd + 2, cols(n)], ALU.mult)
                    V.drain().then_inc(L.Dy.sem, 1)

                def lows(n, qd, cq):
                    p = qd % 2
                    dve.wait_ge(*L.Hh.at(cq + 1))
                    V.tensor_tensor(L.y_lo[:, 2 * qd:2 * qd + 2, cols(n)], L.yt[:, p],
                                    L.y_hi[:, 2 * qd:2 * qd + 2, cols(n)], ALU.subtract)
                    V.drain()

                def block_step(n, first=False, last=False):
                    for qd in range(4):
                        cq = 4 * n + qd
                        normals(qd, cq)
                        if not (last and qd == 3):
                            maxima(n + (qd + 1) // 4, (qd + 1) % 4, cq + 1)
                        if not (last and qd >= 1):
                            stage_q(n + (qd + 3) // 4, (qd + 3) % 4, cq + 3)
                        if not (first and qd == 0):
                            outputs(n if qd else n - 1, (qd + 3) % 4, cq - 1)
                            stage_v(n, qd, cq)
                        if not (first and qd < 2):
                            lows(n if qd >= 2 else n - 1, (qd + 2) % 4, cq - 2)

                V.memset(L.qs[:], 0.0)
                V.drain()
                stage_q(0, 0, 0)
                stage_q(0, 1, 1)
                stage_v(0, 0, 0)
                maxima(0, 0, 0)
                stage_q(0, 2, 2)
                block_step(0, first=True)
                with dve.Fori(1, NBLK - 1) as n:
                    block_step(n)
                block_step(NBLK - 1, last=True)
                outputs(NBLK - 1, 3, 4 * NBLK - 1)
                lows(NBLK - 1, 2, 4 * NBLK - 2)
                lows(NBLK - 1, 3, 4 * NBLK - 1)
                V.memset(L.qz[:], 0.0)
                V.drain()
                for half in range(2):
                    rows = slice(HD * half, HD * half + HD)
                    V.tensor_copy(L.qz[rows].rearrange("p b (t r) -> p b t r", r=2)[:, :, :, half],
                                  L.q[rows, :, T:NT].rearrange("p t b -> p b t"))
                V.tensor_copy(L.kc[:, :, :, WIN], L.kd[:, :, P + T:P + NT])
                V.drain().then_inc(L.zs.sem, 1)
                dve.wait_ge(*L.ssS.at(1))
                W1 = WIN + 1
                V.tensor_scalar(L.ss[0:8, 0:15, :].rearrange("p (a b) n -> p a (b n)", b=3), ps[0:8, 0:5, 0:3 * W1],
                                SCALE, None, ALU.mult)
                V.tensor_scalar(L.ss[0:8, 15, :], ps[0:8, 5, 0:W1], SCALE, None, ALU.mult)
                V.drain()
                V.tensor_reduce(L.sm[0:8, 0], L.ss[0:8], AX.X, ALU.max)
                V.drain()
                V.tensor_tensor(L.sm[0:8, 0], L.sm[0:8, 0], L.sk[0:8], ALU.max)
                V.drain()
                V.tensor_tensor(L.ss[0:8], L.ss[0:8], L.sm[0:8, 0].rearrange("p (e o) -> p e o", o=1).to_broadcast([8, 16, W1]),
                                ALU.subtract)
                V.tensor_tensor(L.sm[0:8, 2], L.sk[0:8], L.sm[0:8, 0], ALU.subtract)
                V.drain().then_inc(L.ssE.sem, 1)
                dve.wait_ge(*L.ssX.at(1))
                V.tensor_reduce(L.sm[0:8, 1], L.ss[0:8], AX.X, ALU.add)
                V.drain()
                V.tensor_tensor(L.sm[0:8, 1], L.sm[0:8, 1], L.sm[0:8, 2], ALU.add)
                V.drain()
                V.reciprocal(L.sm[0:8, 3], L.sm[0:8, 1])
                V.drain()
                V.tensor_tensor(L.ss[0:8], L.ss[0:8], L.sm[0:8, 3].rearrange("p (e o) -> p e o", o=1).to_broadcast([8, 16, W1]),
                                ALU.mult)
                V.drain().then_inc(L.ssN.sem, 1)
                dve.wait_ge(*L.ssT.at(1))
                V.tensor_copy(L.pts[:], ps[:, 6, 0:P])
                V.tensor_copy(L.po[0:16], ps[0:16, 7, 0:8])
                V.drain()
                V.tensor_tensor(L.zo[0:16], L.po[0:16].rearrange("p (o h) -> p o h", o=1).to_broadcast([16, 16, NS]),
                                L.dx[0:16], ALU.mult)
                V.drain().then_inc(L.ssP.sem, 1)
                dve.wait_ge(*L.ssO.at(1))
                for kv in range(2):
                    src = ps[HD * kv:HD * kv + HD, 0, 0:P].rearrange("p (b k t r) -> p k r t b", b=NS, k=2, t=4)
                    for half in range(2):
                        rows = slice(HD * half, HD * half + HD)
                        V.tensor_tensor(L.ys[rows, 4 * kv:4 * kv + 4, :], src[:, kv, half], L.gate[rows, 4 * kv:4 * kv + 4, T:NT],
                                        ALU.mult)
                V.drain().then_inc(L.ssY.sem, 1)
                dve.wait_ge(*L.ssH.at(1))
                V.tensor_tensor(L.y_lo[:, :, T:NT], L.ys[:], L.y_hi[:, :, T:NT], ALU.subtract)
                V.drain().then_inc(L.y_lo_done.sem, 1)
                yssq(L)

            def layer_c(L):
                r = L.r0
                dve.wait_ge(*L.sp_e.at(1))
                V.tensor_scalar(L.sp[:, 2], L.sp[:, 0], 2.0, None, ALU.add)
                V.drain()
                V.reciprocal(L.sp[:, 2], L.sp[:, 2])
                V.drain()
                V.tensor_tensor(L.sp[:, 2], L.sp[:, 2], L.sp[:, 0], ALU.mult)
                V.drain()
                V.tensor_tensor(L.sp[:, 3], L.sp[:, 2], L.sp[:, 2], ALU.mult)
                V.memset(L.sp[:, 4], 1.0 / 17)
                V.drain()
                for d in (15, 13, 11, 9, 7, 5, 3, 1):
                    V.tensor_tensor(L.sp[:, 4], L.sp[:, 4], L.sp[:, 3], ALU.mult)
                    V.drain()
                    V.tensor_scalar(L.sp[:, 4], L.sp[:, 4], 1.0 / d, None, ALU.add)
                    V.drain()
                V.tensor_tensor(L.sp[:, 4], L.sp[:, 4], L.sp[:, 2], ALU.mult)
                V.tensor_scalar(L.sp[:, 5], cvec[:, 7], -1.0, 0.0, ALU.mult, ALU.max)
                V.drain()
                V.tensor_scalar(L.sp[:, 4], L.sp[:, 4], 8.0, None, ALU.mult)
                V.drain()
                V.scalar_tensor_tensor(L.sp[:, 1], L.sp[:, 5], 4.0, L.sp[:, 4], ALU.mult, ALU.add)
                V.drain().then_inc(L.sp_done.sem, 1)
                V.memset(L.xr[:, 0:CONV - 1], 0.0)
                dve.wait_ge(*L.c_in.at(32))

                def tap(t, m):
                    return col_of(cvec, t, m)

                def conv(m, slot):
                    read(L.xr[:, CONV - 1:CONV - 1 + NT], slot, m + (r + 1))
                    st = L.st[:, m] if isinstance(m, int) else L.st[:, bass.ds(m, 1)].rearrange("p o t b -> p (o t) b")
                    V.tensor_copy(st[:, CONV - 1, :], L.xr[:, CONV - 1 + T:CONV - 1 + NT])
                    V.tensor_copy(tile_of(L.cp, m), L.xr[:, T:T + CONV - 1])
                    out = tile_of(L.xc, m)
                    V.tensor_scalar(out[:, 0:T], L.xr[:, 0:T], tap(0, m), tap(4, m), ALU.mult, ALU.add)
                    V.tensor_scalar(out[:, T:NT], st[:, 0, :], tap(0, m), tap(4, m), ALU.mult, ALU.add)
                    V.drain()
                    for t in range(1, CONV):
                        V.scalar_tensor_tensor(out[:, 0:T], L.xr[:, t:t + T], tap(t, m), out[:, 0:T], ALU.mult, ALU.add)
                        V.scalar_tensor_tensor(out[:, T:NT], st[:, t, :], tap(t, m), out[:, T:NT], ALU.mult, ALU.add)
                        V.drain()

                with dve.Fori(0, KT // 2) as i:
                    for j in range(2):
                        conv(2 * i + j, j)
                V.drain().then_inc(L.conv_done.sem, 1)

                def chain(m):
                    rt, it = L.rt[:, m % 2, :], L.it[:, m % 2, :]
                    dve.wait_ge(*L.th.at(m + 1))
                    V.tensor_scalar(L.dn[:], rt, 1.0, None, ALU.add)
                    V.tensor_tensor(it, it, L.xc[:, m, :], ALU.mult)
                    V.drain()
                    V.reciprocal(L.dn[:], L.dn[:])
                    V.drain()
                    dve.wait_ge(*L.root2.at(m + 1))
                    V.tensor_scalar(rt, L.dn[:], 2.0, -1.0, ALU.mult, ALU.add)
                    V.scalar_tensor_tensor(L.rc[:], L.rc[:], 2.0, L.dn[:], ALU.mult, ALU.mult)
                    V.drain()
                    V.memset(L.rc[:, 0:1], 1.0)
                    V.drain()
                    V.tensor_tensor(it, it, L.rc[:], ALU.mult)
                    V.drain()
                    V.tensor_tensor_scan(L.hs[:, 0:T], rt[:, 0:T], it[:, 0:T], 0.0, ALU.mult, ALU.add)
                    V.tensor_tensor(L.hs[:, T:NT], rt[:, T:NT], L.h0[:, m, :], ALU.mult)
                    V.drain()
                    V.tensor_tensor(L.hs[:, T:NT], L.hs[:, T:NT], it[:, T:NT], ALU.add)
                    V.drain().then_inc(L.used.sem, 1)
                    V.tensor_copy(L.hp[:, m:m + 1], L.hs[:, T - 1:T])
                    V.tensor_copy(L.hn[:, m, :], L.hs[:, T:NT])
                    V.drain()
                    dve.wait_ge(*L.g_act.at(m + 1))
                    V.tensor_tensor(L.hs[:], L.hs[:], L.gate[:, m, :], ALU.mult)
                    V.drain().then_inc(L.y_done.sem, 1)
                    dve.wait_ge(*L.y_hi_done.at(m + 1))
                    V.tensor_tensor(L.y_lo[:, m, :], L.hs[:], L.y_hi[:, m, :], ALU.subtract)
                    V.drain().then_inc(L.y_lo_done.sem, 1)

                for n in range(4):
                    for t in range(2):
                        dve.wait_ge(*L.xh.at(2 * n + t + 1))
                        V.tensor_tensor(L.xc_lo[t][:], L.xc[:, 2 * n + t, :], L.xc_hi[:, t, :], ALU.subtract
                                        ).then_inc(L.xsplit.sem, 1)
                    for t in range(2):
                        m = 2 * n + t
                        if n:
                            chain(m - 2)
                        read(L.gate[:, m, :], t, L.result_of(L.u0 + KT + 3 * n + t) + 1)
                        V.drain().then_inc(L.in_done.sem, 1)
                chain(KT - 2)
                chain(KT - 1)
                yssq(L)

            prev = None
            for L in layers:
                pre(L, prev)
                (layer_a if L.kind == "a" else layer_b if L.kind == "b" else layer_c)(L)
                prev = L
            for k in range(KT):
                new_x(prev, k)


INS = {
    "xt": (KT, P, NT), "wu": (N_UNITS, P, 8 * P), "ident": (P, P), "tri": (P, P),
    "g_pre": (P, 4, KT), "g_post": (P, 4, KT), "ln_g": (P, 2, MA), "ln_b": (P, 2, MA), "cvec": (P, 8, KT),
    "wst": (2, P, 4, P), "bs": (2, 4, P), "corner": (2, 4),
    "cos": (P, NT), "sin": (P, NT), "sink": (1, NH), "sink8": (8, 2 * NS), "mask": (P, 2, 2 * WIN), "dx": (2 * NS, 2 * NS, NS),
    "kct": (P, WIN, NS), "kcd": (P, 2, NS, WIN), "vct": (NS, WIN, P),
    "st": (P, KT, CONV - 1, NS), "h0": (P, KT, NS),
}
OUTS = {
    "y": (KT, P, NT), "av": (2, P, MA, NS), "kp": (P, WIN), "vp": (WIN, P), "ks": (P, WIN, NS), "vs": (NS, WIN, P),
    "ccp": (P, KT, CONV - 1), "chp": (P, KT), "ccs": (P, KT, CONV - 1, NS), "chs": (P, KT, NS),
}


def shape_constants():
    row = np.arange(P)
    half = HD // 2
    inv = np.float32(10000.0) ** (-np.arange(half, dtype=np.float32) / np.float32(half))
    pos = np.concatenate([np.arange(T), np.full(NS, 1024)]).astype(np.float32)
    angle = (pos[None, :] * inv[row % half][:, None]).astype(np.float32)
    sign = np.where(row % HD < half, -1.0, 1.0).astype(np.float32)[:, None]
    q, s = np.arange(WIN)[:, None], np.arange(2 * WIN)[None, :]
    seen = (s - WIN <= q) & (q - (s - WIN) <= WIN)
    mask = np.stack([np.where(seen & (s >= WIN), 0.0, NEG), np.where(seen, 0.0, NEG)], axis=1)
    return {
        "ident": np.eye(P, dtype=np.float32),
        "tri": (row[:, None] <= row[None, :]).astype(np.float32),
        "cos": np.cos(angle), "sin": np.sin(angle) * sign,
        "mask": mask.astype(np.float32),
        "dx": np.repeat(np.eye(2 * NS, dtype=np.float32)[:, :, None], NS, axis=2),
    }


def by_units(w):
    return w.reshape(8, P, -1, P).transpose(2, 1, 0, 3).reshape(-1, P, 8 * P)


def by_features(v):
    return np.moveaxis(v.reshape(v.shape[:-1] + (-1, P)), -1, 0)


def lay_out(i):
    units = []
    for j, kind in ((0, "a"), (0, "b"), (0, "c"), (1, "a")):
        if kind == "a":
            w = by_units(i["a_w_in"][j])
            u, v, g = w[:MA], w[MA:2 * MA], w[2 * MA:]
            units += [v, np.stack([u, g], axis=1).reshape(-1, P, 8 * P)]
            units += [by_units(i["a_w_out"][j][:D]), by_units(i["a_w_out"][j][D:])]
        elif kind == "b":
            w = by_units(i["b_w_in"][0])
            units += [w[KT:KT + 2], w[:KT], w[KT + 2:], by_units(i["b_w_out"][0])]
        else:
            w = by_units(i["c_w_in"][0])
            ax = np.stack([i["c_w_a"][0], i["c_w_x"][0]]).reshape(2, 4, 2, P, 2, P)
            gates = ax.transpose(1, 3, 4, 0, 2, 5).reshape(4, 1, P, 8 * P)
            units += [w[:KT], np.concatenate([w[KT:].reshape(4, 2, P, 8 * P), gates], axis=1).reshape(-1, P, 8 * P)]
            units.append(by_units(i["c_w_out"][0]))
    xall = np.concatenate([i["x_prompt"][0], i["x_sample"][:, 0]], axis=0)
    kct = i["cache_b_k"][0].transpose(2, 3, 0, 1)
    cvec = np.concatenate([i["c_conv_w"][0], i["c_conv_b"], i["c_b_a"], i["c_b_x"], i["c_lam"]], axis=0)
    sinks = i["b_sinks"].reshape(2, 8)
    return {
        "xt": xall.T.reshape(KT, P, NT),
        "wu": np.concatenate(units, axis=0),
        "g_pre": by_features(i["norm_pre"]), "g_post": by_features(i["norm_post"]),
        "ln_g": by_features(i["a_ln_g"]), "ln_b": by_features(i["a_ln_b"]), "cvec": by_features(cvec),
        "wst": i["a_w_s"].transpose(0, 3, 1, 2), "bs": i["a_b_s"], "corner": i["a_w_s"][:, :, 0, 0],
        "sink": i["b_sinks"], "sink8": np.tile(sinks.T, (1, NS)),
        "kct": kct.transpose(0, 1, 3, 2).reshape(P, WIN, NS),
        "kcd": np.concatenate([kct, kct], axis=1).transpose(1, 0, 2, 3),
        "vct": i["cache_b_v"][0].reshape(NS, WIN, P),
        "st": by_features(i["state_c_conv"][0]).transpose(0, 3, 2, 1),
        "h0": by_features(i["state_c_h"][0]).transpose(0, 2, 1),
        **shape_constants(),
    }


def kernel(**inputs):
    import concourse.bacc as bacc
    from concourse.bass_utils import run_bass_kernel_spmd

    nc = bacc.Bacc("TRN2", target_bir_lowering=False, num_devices=1)
    laid = lay_out({k: np.asarray(v) for k, v in inputs.items()})
    io, arrays = {}, {}
    for name, shape in INS.items():
        arrays["in_" + name] = np.ascontiguousarray(laid[name])
        assert arrays["in_" + name].shape == shape, (name, arrays["in_" + name].shape, shape)
        io[name] = nc.dram_tensor("in_" + name, shape, F32, kind="ExternalInput").ap()
    for name, shape in OUTS.items():
        io[name] = nc.dram_tensor("out_" + name, shape, F32, kind="ExternalOutput").ap()
    io["x_save"] = nc.dram_tensor("x_save", (KT, P, NT), F32, kind="Internal").ap()
    build(nc, io)
    run = run_bass_kernel_spmd(nc, [arrays], core_ids=[0])
    o = {name: run.results[0]["out_" + name] for name in OUTS}
    y = o["y"].reshape(D, NT)

    def heads(a):
        return a.reshape(a.shape[:-1] + (NKV, HD))

    return (
        np.ascontiguousarray(y[:, :T].T)[None],
        np.ascontiguousarray(y[:, T:].T)[:, None],
        np.ascontiguousarray(o["av"].transpose(0, 3, 2, 1).reshape(2, NS, 1, DA)),
        np.ascontiguousarray(heads(o["kp"].T)[None, None]),
        np.ascontiguousarray(heads(o["vp"])[None, None]),
        np.ascontiguousarray(heads(o["ks"].transpose(2, 1, 0))[None]),
        np.ascontiguousarray(heads(o["vs"])[None]),
        np.ascontiguousarray(o["ccp"].transpose(2, 1, 0).reshape(1, 1, CONV - 1, D)),
        np.ascontiguousarray(o["chp"].T.reshape(1, 1, D)),
        np.ascontiguousarray(o["ccs"].transpose(3, 2, 1, 0).reshape(1, NS, CONV - 1, D)),
        np.ascontiguousarray(o["chs"].transpose(2, 1, 0).reshape(1, NS, D)),
    )
```

```python
from contextlib import ExitStack

import numpy as np

import concourse.bass as bass
from concourse import mybir

F32 = mybir.dt.float32
F32R = mybir.dt.float32r
ALU = mybir.AluOpType
ACT = mybir.ActivationFunctionType
AX = mybir.AxisListType

P = 128
D = 1024
KT = D // P
T = 1024
NS = 8
NT = T + NS
CH = 3
CW = NT // CH
TILE = NT * 4
DA = 2048
MA = DA // P
NH, HD, NKV = 16, 64, 2
WIN = 128
NBLK = T // WIN
CONV = 4
NEG = -1e30
SCALE = HD ** -0.5
A_EARLY = 3
N_UNITS = (3 * MA + 2 * KT) * 2 + (2 * KT + 2 + KT) + (2 * KT + 4 + KT)


class Counts:

    def __init__(self):
        self.unit = 0
        self.result = 0

    def take(self, units, results):
        at = self.unit, self.result
        self.unit += units
        self.result += results
        return at


class Signal:

    def __init__(self, sem, base):
        self.sem, self.base = sem, base

    def at(self, n):
        return self.sem, n + self.base


PER_LAYER = {
    "hi_done": (KT, KT, KT), "h_done": (KT, KT, KT), "sq_done": (KT, KT, KT), "sq_used": (KT - 2, KT - 2, KT - 2),
    "ssq_mm": (2, 2, 2), "root": (2, 2, 2), "rx_done": (1, 1, 1),
    "x_saved": (16 * KT,) * 3, "x_back": (16 * KT,) * 3, "in_done": (3 * MA, 2 * KT + 2, KT), "act_done": (MA, KT, 0),
    "y_hi_done": (0, 0, KT), "y_lo_done": (0, 1, KT), "y_even": (KT, 0, 0), "y_odd": (KT, 0, 0), "ug_done": (1, 0, 0), "acc_done": (KT, 0, 0), "ysq_done": (KT, KT, KT),
    "yssq_done": (KT - 1,) * 3, "yssq_mm": (2, 2, 2), "yroot": (2, 2, 2), "x_new": (KT, KT, KT),
    "rp_done": (1, 1, 1), "scaled": (KT - 1,) * 3,
    "ws_in": (64, 0, 0), "wm": (1, 0, 0), "wh": (1, 0, 0), "ws_done": (1, 0, 0), "vsq": (MA, 0, 0),
    "vsum_done": (2 * MA, 0, 0), "stat_mm": (4, 0, 0), "stat": (5, 0, 0), "vst": (MA, 0, 0), "vT": (MA, 0, 0),
    "vTh": (MA, 0, 0), "vTl": (MA, 0, 0), "mix": (MA, 0, 0), "y_done": (MA, 0, KT), "u_act": (MA, 0, 0),
    "g_act": (MA, 0, KT), "tmp_hi": (MA, 0, 0), "lo_cut": (MA, 0, 0), "vout": (16, 0, 0), "var_done": (1, 0, 0),
}


def build(nc, io):
    with ExitStack() as ctx:
        def sem(name):
            return ctx.enter_context(nc.semaphore(name))

        base = (nc.sbuf_base + 31) // 32 * 32
        W_AT = base
        X_AT = W_AT + 3 * 2 * 4096
        R_AT = [X_AT + KT * TILE, X_AT + KT * TILE + MA * TILE]
        S_AT = R_AT[1] + MA * TILE
        END = nc.sbuf_usable_end

        def at(name, offset, shape, dtype=F32):
            size = 4
            for n in shape[1:]:
                size *= n
            assert offset + size <= END, (name, offset + size - END)
            return nc.alloc_sbuf_tensor_at(name, shape, dtype, offset=offset)

        small = [S_AT]

        def keep(name, shape, dtype=F32):
            size = 4
            for n in shape[1:]:
                size *= n
            o = small[0]
            small[0] += (size + 31) // 32 * 32
            return at(name, o, shape, dtype)

        w_raw = at("w_raw", W_AT, [P, 2, 8, P])
        w_hi = at("w_hi", W_AT + 8192, [P, 2, 8, P], F32R)
        w_lo = at("w_lo", W_AT + 16384, [P, 2, 8, P], F32R)
        x = at("x", X_AT, [P, KT, NT])
        rx = keep("rx", [P, NT])
        sq_at = small[0]
        sqt = keep("sqt", [P, NT])
        ssq = keep("ssq", [P, NT])
        sq2 = at("sq2", sq_at, [P, 2, NT])
        vt_hi = at("vt_hi", sq_at, [P, NBLK, P], F32R)
        vt_lo = at("vt_lo", sq_at + TILE, [P, NBLK, P], F32R)
        ident = keep("ident", [P, P])
        ones = keep("ones", [P, P])
        zero = keep("zero", [P, 8])
        g_pre = keep("g_pre", [P, 4, KT])
        g_post = keep("g_post", [P, 4, KT])
        ln_g = keep("ln_g", [P, 2, MA])
        ln_b = keep("ln_b", [P, 2, MA])
        cvec = keep("cvec", [P, 8, KT])
        eps = keep("eps", [P, 2])
        cell_act, cell_dve = keep("cell_act", [P, 8]), keep("cell_dve", [P, 8])
        a_at = small[0]
        v_new = keep("v_new", [P, MA, NS])
        bs_at = small[0]
        bs_bc = keep("bs_bc", [P, 4, P])
        corner = keep("corner", [P, 4])
        ps = ctx.enter_context(nc.psum_tensor("ps", [P, 8, 512], F32))

        w_loaded = [sem("w_loaded0"), sem("w_loaded1")]
        w_hi_done, w_lo_done = sem("w_hi_done"), sem("w_lo_done")
        result = sem("result")
        evac = [sem("evac0"), sem("evac1")]
        consts = sem("consts")
        setup = sem("setup")
        x_in = [sem(f"x_in{k}") for k in range(KT)]
        gains = sem("gains")
        n_consts = 5
        c = Counts()

        class Layer:
            pass

        layers = []
        shared = {}
        for i, kind in enumerate("abca"):
            L = Layer()
            L.i, L.kind, L.j = i, kind, i // 3
            hreg = [0, 1, 0, 1][i]
            H_AT, O_AT = R_AT[hreg], R_AT[1 - hreg]
            n = f"l{i}_"

            def s(name, i=i, kind=kind):
                if name not in shared:
                    shared[name] = sem(name)
                before = sum(PER_LAYER[name]["abc".index(k)] for k in "abca"[:i]) if name in PER_LAYER else 0
                return Signal(shared[name], before)

            L.h_hi = at(n + "h_hi", H_AT, [P, KT, NT], F32R)
            L.h_lo = at(n + "h_lo", H_AT + KT * TILE, [P, KT, NT], F32R)
            L.hi_done, L.h_done, L.sq_done = s("hi_done"), s("h_done"), s("sq_done")
            L.sq_used, L.ssq_mm, L.root, L.rx_done = s("sq_used"), s("ssq_mm"), s("root"), s("rx_done")
            L.rp_done, L.scaled = s("rp_done"), s("scaled")
            L.x_saved, L.x_back = s("x_saved"), s("x_back")
            L.in_done, L.act_done = s("in_done"), s("act_done")
            L.y_hi_done, L.y_lo_done = s("y_hi_done"), s("y_lo_done")
            L.acc_done, L.ysq_done, L.yssq_done = s("acc_done"), s("ysq_done"), s("yssq_done")
            L.yssq_mm, L.yroot, L.x_new = s("yssq_mm"), s("yroot"), s("x_new")
            if kind == "a":
                L.u0, L.r0 = c.take(3 * MA + 2 * KT, 3 * MA + 2 * KT)
                L.v = at(n + "v", O_AT, [P, MA, NT])
                L.y = L.v
                L.y_hi = at(n + "y_hi", O_AT, [P, MA, NT], F32R)
                L.y_lo = at(n + "y_lo", H_AT, [P, KT, NT], F32R)
                L.acc = at(n + "acc", H_AT + KT * TILE, [P, KT, NT])
                L.tmp = at(n + "tmp", X_AT, [P, 2, NT])
                L.ug = at(n + "ug", X_AT + 2 * TILE, [P, NT])
                L.vstage = at(n + "vstage", X_AT + 3 * TILE, [P, NT])
                L.mu = at(n + "mu", X_AT + 4 * TILE, [P, NT])
                L.rstd = at(n + "rstd", X_AT + 5 * TILE, [P, NT])
                L.vsum = at(n + "vsum", X_AT + 6 * TILE, [P, NT])
                L.wsr = at(n + "wsr", X_AT + 2 * TILE, [P, 4, P])
                L.tri = at(n + "tri", X_AT + 3 * TILE, [P, P])
                L.ws_hi = at(n + "ws_hi", X_AT + 7 * TILE, [P, 4, P], F32R)
                L.ws_lo = at(n + "ws_lo", X_AT + 7 * TILE + 2048, [P, 4, P], F32R)
                L.y_tmp = [at(n + "y_tmp0", X_AT + 6 * TILE, [P, NT], F32R), at(n + "y_tmp1", X_AT + TILE, [P, NT], F32R)]
                L.y_lo_x = at(n + "y_lo_x", X_AT + 2 * TILE, [P, A_EARLY, NT], F32R)
                L.y_even, L.y_odd, L.ug_done = s("y_even"), s("y_odd"), s("ug_done")
                L.ws_in, L.wm, L.wh, L.ws_done = s("ws_in"), s("wm"), s("wh"), s("ws_done")
                L.vsq, L.vsum_done = s("vsq"), s("vsum_done")
                L.stat_mm, L.stat = s("stat_mm"), s("stat")
                L.vst, L.vT, L.vTh, L.vTl, L.mix, L.y_done = (
                    s("vst"), s("vT"), s("vTh"), s("vTl"), s("mix"), s("y_done"))
                L.u_act, L.g_act = s("u_act"), s("g_act")
                L.tmp_hi, L.lo_cut = s("tmp_hi"), s("lo_cut")
                L.vout, L.var_done = s("vout"), s("var_done")
            if kind == "b":
                L.u0, L.r0 = c.take(2 * KT + 2 + KT, 2 * KT + 2 + KT)
                L.q = at(n + "q", O_AT, [P, KT, NT])
                L.gate = at(n + "gate", O_AT + KT * TILE, [P, KT, NT])
                L.vf = at(n + "vf", O_AT + KT * TILE, [P, NT])
                L.y_hi = at(n + "y_hi", O_AT, [P, KT, NT], F32R)
                L.y_lo = at(n + "y_lo", O_AT + KT * TILE, [P, KT, NT], F32R)
                L.acc = at(n + "acc", H_AT, [P, KT, NT])
                o = X_AT
                L.kd = at(n + "kd", o, [P, 2, P + NT]); o += 2 * (P + NT) * 4
                L.vtok = at(n + "vtok", o, [P, NBLK + 1, P]); o += (NBLK + 1) * P * 4
                L.cos = at(n + "cos", o, [P, NT]); o += TILE
                L.sin = at(n + "sin", o, [P, NT]); o += TILE
                L.kf = at(n + "kf", o, [P, NT]); o += TILE
                L.sw = at(n + "sw", o, [P, NT]); o += TILE
                L.vfs = at(n + "vfs", o, [P, 2 * NS]); o += 64
                L.v16 = at(n + "v16", o, [P, P]); o += 512
                L.sink = at(n + "sink", o, [P, NH]); o += 64
                assert o <= X_AT + KT * TILE
                o = H_AT
                L.qs = at(n + "qs", o, [P, 2, 4, P]); o += 4096
                L.vs = at(n + "vs", o, [P, 2, 2, P]); o += 2048
                L.sc = at(n + "sc", o, [P, 4, 4, 2 * WIN]); o += 16384
                L.pt = at(n + "pt", o, [P, 2, 2, 4 * P]); o += 8192
                L.yt = at(n + "yt", o, [P, 2, 2, P]); o += 2048
                L.mask = at(n + "mask", bs_at, [P, 2, 2 * WIN])
                L.mx = at(n + "mx", o, [P, 2, 4, 4]); o += 128
                L.rq = at(n + "rq", o, [P, 4, 4]); o += 64
                L.kc = at(n + "kc", o, [P, 2, NS, WIN + 1]); o += 2 * NS * (WIN + 1) * 4
                L.vc = at(n + "vc", o, [P, NS, P]); o += 4096
                L.qz = at(n + "qz", o, [P, NS, NH]); o += 512
                L.ss = at(n + "ss", o, [P, 2 * NS, WIN + 1]); o += 2 * NS * (WIN + 1) * 4
                L.sk = at(n + "sk", o, [P, 2 * NS]); o += 64
                L.sm = at(n + "sm", o, [P, 5, 2 * NS]); o += 320
                L.pts = at(n + "pts", o, [P, P]); o += 512
                L.po = at(n + "po", o, [P, NS]); o += 32
                L.dx = at(n + "dx", o, [P, 2 * NS, NS]); o += 512
                L.zo = at(n + "zo", o, [P, 2 * NS, NS]); o += 512
                L.ys = at(n + "ys", o, [P, KT, NS]); o += 256
                assert o <= H_AT + MA * TILE
                L.Rq, L.rope_in, L.sw_done, L.k_rot, L.vf_done, L.v_tr = s("Rq"), s("rope_in"), s("sw_done"), s("k_rot"), s("vf_done"), s("v_tr")
                L.vfs_done, L.vtok_done, L.kout, L.at_in, L.stq, L.stv = s("vfs_done"), s("vtok_done"), s("kout"), s("at_in"), s("stq"), s("stv")
                L.S, L.B, L.X, L.C, L.TP, L.PC = s("S"), s("B"), s("X"), s("C"), s("TP"), s("PC")
                L.PV, L.Dy, L.Hh, L.zs, L.ssS, L.ssE = s("PV"), s("Dy"), s("Hh"), s("zs"), s("ssS"), s("ssE")
                L.ssX, L.ssN, L.ssT, L.ssP, L.ssO, L.ssY = s("ssX"), s("ssN"), s("ssT"), s("ssP"), s("ssO"), s("ssY")
                L.ssH, L.ss_read, L.kset = s("ssH"), s("ss_read"), s("kset")
            if kind == "c":
                L.u0, L.r0 = c.take(2 * KT + 4 + KT, 2 * KT + 16 + KT)

                def result_of(u, L=L):
                    n, t = divmod(u - L.u0 - KT, 3)
                    if n >= 4:
                        return L.r0 + KT + 24 + (u - L.u0 - KT - 12)
                    return L.r0 + KT + 6 * n + (0, 4, 5)[t] if n >= 0 else L.r0 + u - L.u0

                def g_result(m, L=L):
                    return L.r0 + KT + 3 * m + (2 if m % 2 else 0)

                L.result_of, L.g_result = result_of, g_result
                L.xc = at(n + "xc", O_AT, [P, KT, NT])
                L.gate = at(n + "gate", O_AT + KT * TILE, [P, KT, NT])
                L.y_hi = at(n + "y_hi", O_AT, [P, KT, NT], F32R)
                L.y_lo = at(n + "y_lo", O_AT + KT * TILE, [P, KT, NT], F32R)
                L.acc = at(n + "acc", H_AT, [P, KT, NT])
                o = X_AT
                L.xc_hi = at(n + "xc_hi", sq_at, [P, 2, NT], F32R)
                L.xr = at(n + "xr", o, [P, CONV - 1 + NT])
                L.xc_lo = [at(n + "xc_lo0", o, [P, NT], F32R), at(n + "xc_lo1", a_at, [P, NT], F32R)]
                o += (CONV - 1 + NT + 5) * 4
                L.st = at(n + "st", o, [P, KT, CONV, NS]); o += KT * CONV * NS * 4
                L.h0 = at(n + "h0", o, [P, KT, NS]); o += KT * NS * 4
                L.cp = at(n + "cp", o, [P, KT, CONV - 1]); o += 96
                L.hp = at(n + "hp", o, [P, KT]); o += 32
                L.hn = at(n + "hn", o, [P, KT, NS]); o += 256
                L.sp = at(n + "sp", o, [P, 6, KT]); o += 192
                o += -o % 32
                L.rt = at(n + "rt", o, [P, 2, NT]); o += 2 * TILE
                L.it = at(n + "it", o, [P, 2, NT]); o += 2 * TILE
                L.rc = [at(n + "rc0", o, [P, NT]), at(n + "rc1", a_at + TILE, [P, NT])]
                o += TILE
                L.hs = at(n + "hs", o, [P, NT]); o += TILE
                assert o <= X_AT + KT * TILE
                L.c_in, L.sp_e, L.sp_done, L.conv_done, L.g_act, L.xh = s("c_in"), s("sp_e"), s("sp_done"), s("conv_done"), s("g_act"), s("xh")
                L.xsplit, L.sig, L.ix, L.root2, L.used, L.y_done = s("xsplit"), s("sig"), s("ix"), s("root2"), s("used"), s("y_done")
                L.cout, L.th, L.pm = s("cout"), s("th"), s("pm")
            layers.append(L)
        assert c.unit == N_UNITS
        final = sem("final")

        STAT = [(5, 504, T, NS), (6, 0, 0, 512), (7, 0, 512, 512)]
        POST_STAT = [(2, 504, T, NS), (6, 0, 0, 512), (7, 0, 512, 512)]

        def psum_result(slot):
            return ps[:, 3 * slot:3 * slot + 3, 0:CW]

        def chunks(ap):
            return ap.rearrange("p (c n) -> p c n", c=CH)

        def tile_of(t, m):
            if isinstance(m, int):
                return t[:, m, :]
            return t[:, bass.ds(m, 1), :].rearrange("p o n -> p (o n)")

        def col_of(t, j, m):
            if isinstance(m, int):
                return t[:, j, m:m + 1]
            return t[:, j, bass.ds(m, 1)]

        block = ctx.enter_context(nc.Block())

        @block.sync
        def _(sp):
            sp.dma_start(w_raw[:, 0], io["wu"][0].rearrange("p (k m) -> p k m", m=P)).then_inc(w_loaded[0], 16)
            for k in range(KT):
                sp.dma_start(x[:, k, :], io["xt"][k]).then_inc(x_in[k], 16)
            sp.dma_start(w_raw[:, 1], io["wu"][1].rearrange("p (k m) -> p k m", m=P)).then_inc(w_loaded[1], 16)
            with sp.Fori(1, N_UNITS // 2) as i:
                for j in range(2):
                    sp.wait_ge(w_lo_done, 2 * i + (j - 1))
                    sp.dma_start(w_raw[:, j], io["wu"][bass.ds(2 * i + j, 1)].rearrange("o p (k m) -> p (o k) m", m=P)
                                 ).then_inc(w_loaded[j], 16)

        @block.gpsimd
        def _(pool):
            zeros = zero[:, 0:1].to_broadcast([P, 8 * P])

            def split(j, loaded, n):
                pool.wait_ge(w_loaded[j], loaded)
                nc.gpsimd.tensor_tensor(w_hi[:, j].rearrange("p k m -> p (k m)"), w_raw[:, j].rearrange("p k m -> p (k m)"),
                                        zeros, ALU.add).then_inc(w_hi_done, 1)
                pool.wait_ge(w_hi_done, n + 1)
                nc.gpsimd.tensor_tensor(w_lo[:, j].rearrange("p k m -> p (k m)"), w_raw[:, j].rearrange("p k m -> p (k m)"),
                                        w_hi[:, j].rearrange("p k m -> p (k m)"), ALU.subtract).then_inc(w_lo_done, 1)

            pool.wait_ge(setup, 1)
            for j in range(2):
                split(j, 16, j)
            def refill(first, last, extra):
                with pool.Fori(first // 2, last // 2) as i:
                    for j in range(2):
                        pool.wait_ge(result, 2 * i + (j - 1 + extra))
                        split(j, 16 * i + 16, 2 * i + j)

            def scale(L):
                pool.wait_ge(*L.rp_done.at(1))
                for k in range(1, KT):
                    nc.gpsimd.tensor_tensor(L.acc[:, k, :], L.acc[:, k, :], rx[:], ALU.mult).then_inc(L.scaled.sem, 1)

            def normals(L):
                def quad(qd, cq):
                    pool.wait_ge(*L.Rq.at(cq + 1))
                    nc.gpsimd.tensor_tensor(L.sc[:, qd], L.sc[:, qd],
                                            L.rq[:, qd].rearrange("p (h o) -> p h o", o=1).to_broadcast([P, 4, 2 * WIN]),
                                            ALU.mult).then_inc(L.C.sem, 1)

                with pool.Fori(0, NBLK) as n:
                    for qd in range(4):
                        quad(qd, 4 * n + qd)

            def gate_input(L, m):
                pool.wait_ge(*L.sig.at(m + 1))
                nc.gpsimd.tensor_tensor(L.it[:, m % 2, :], L.it[:, m % 2, :], L.xc[:, m, :], ALU.mult).then_inc(L.ix.sem, 1)

            LA, LB, LC, LZ = layers
            refill(2, LB.u0 + 2, 0)
            scale(LA)
            refill(LB.u0 + 2, LB.u0 + 2 * KT + 4, 0)
            normals(LB)
            refill(LB.u0 + 2 * KT + 4, LC.u0 + 2, 0)
            scale(LB)
            refill(LC.u0 + 2, LC.u0 + KT + 2, 0)
            for u in range(LC.u0 + KT + 2, LC.u0 + 2 * KT + 6):
                n, t = divmod(u - (LC.u0 + KT), 3)
                if t == 0 and 1 <= n <= 4:
                    gate_input(LC, 2 * n - 2)
                pool.wait_ge(result, LC.result_of(u - 2) + 1)
                split(u % 2, 16 * (u // 2) + 16, u)
                if t == 0 and 1 <= n <= 4:
                    gate_input(LC, 2 * n - 1)
            refill(LC.u0 + 2 * KT + 6, LZ.u0 + 2, 12)
            scale(LC)
            refill(LZ.u0 + 2, N_UNITS, 12)
            scale(LZ)

        @block.tensor
        def _(pe):
            def product(slot, w, hi, lo, ready=None, of=range(CH)):
                for k in range(KT):
                    if ready is not None:
                        pe.wait_ge(*ready(k))
                    for t, (wt, mv) in enumerate(((w_hi, hi), (w_hi, lo), (w_lo, hi))):
                        for ch in of:
                            mm = nc.tensor.matmul(ps[:, 3 * slot + ch, 0:CW], wt[:, w, k, :],
                                                  mv[:, k, ch * CW:(ch + 1) * CW],
                                                  start=(k == 0 and t == 0), stop=(k == KT - 1 and t == 2))
                return mm

            def unit(w, slot, u, r, hi, lo, ready=None):
                pe.wait_ge(w_lo_done, u + 1)
                if not (isinstance(r, int) and r < 2):
                    pe.wait_ge(evac[slot], freed(r, slot))
                product(slot, w, hi, lo, ready).then_inc(result, 1)

            def freed(r, slot):
                return r[1] if isinstance(r, tuple) else r // 2

            def units(n, u, r, hi, lo, ready=None):
                for j in range(2):
                    unit((u + j) % 2, (r + j) % 2, u + j, r + j, hi, lo, ready)
                later_units(1, n, u, r, hi, lo)

            def later_units(first, n, u, r, hi, lo):
                if n > 2 * first:
                    with pe.Fori(first, n // 2) as i:
                        for j in range(2):
                            unit((u + j) % 2, (r + j) % 2, 2 * i + (u + j), (None, i + (r + j) // 2), hi, lo)

            def column_sums(src, signal, where=STAT, start=True, stop=True):
                for bank, col, tok, n in where:
                    mm = nc.tensor.matmul(ps[:, bank, col:col + n], ones[:, :], src[:, tok:tok + n], start=start, stop=stop)
                    if bank != 6 and stop:
                        mm.then_inc(signal.sem, 1)

            def first_unit(L):
                pe.wait_ge(w_lo_done, L.u0 + 1)
                if L.r0:
                    pe.wait_ge(evac[0], L.r0 // 2)
                for k in range(KT):
                    pe.wait_ge(*L.hi_done.at(k + 1))
                    for t, (wt, mv) in enumerate(((w_hi, L.h_hi), (w_lo, L.h_hi), (w_hi, L.h_lo))):
                        if t == 2:
                            pe.wait_ge(*L.h_done.at(k + 1))
                        for ch in range(CH):
                            mm = nc.tensor.matmul(ps[:, ch, 0:CW], wt[:, 0, k, :], mv[:, k, ch * CW:(ch + 1) * CW],
                                                  start=(k == 0 and t == 0), stop=(k == KT - 1 and t == 2))
                    if k == KT - 1:
                        mm.then_inc(result, 1)
                    pe.wait_ge(*L.sq_done.at(k + 1))
                    for bank, col, tok, n in STAT:
                        mm = nc.tensor.matmul(ps[:, bank, col:col + n], ones[:, :], sq2[:, k % 2, tok:tok + n],
                                              start=(k == 0), stop=(k == KT - 1))
                        if k == KT - 1 and bank != 6:
                            mm.then_inc(L.ssq_mm.sem, 1)
                    if k < KT - 2:
                        mm.then_inc(L.sq_used.sem, 1)
                pe.wait_ge(*L.root.at(1))

            def post(L, r):
                pe.wait_ge(*L.yssq_done.at(KT - 1))
                pe.wait_ge(evac[0], (r + KT) // 2)
                column_sums(ssq, L.yssq_mm, POST_STAT, stop=False)
                pe.wait_ge(*L.ysq_done.at(KT))
                column_sums(sqt, L.yssq_mm, POST_STAT, start=False)
                pe.wait_ge(*L.yroot.at(1))

            def first_units(n, L, hi, lo):
                u, r = L.u0, L.r0
                first_unit(L)
                unit(1, 1, u + 1, r + 1, hi, lo)
                later_units(1, n, u, r, hi, lo)

            def layer_a(L):
                u, r = L.u0, L.r0
                assert u % 2 == 0 and r % 2 == 0
                first_units(MA, L, L.h_hi, L.h_lo)
                pe.wait_ge(consts, 16 * n_consts)
                u, r = u + MA, r + MA

                def turn(m):
                    pe.wait_ge(*L.vst.at(m + 1))
                    pe.wait_ge(*L.y_done.at(m)) if not (isinstance(m, int) and m == 0) else pe.wait_ge(*L.stat.at(4))
                    for b in range(NBLK):
                        mm = nc.tensor.transpose(ps[:, 6 + b // 4, (b % 4) * P:(b % 4 + 1) * P],
                                                 L.vstage[:, b * P:(b + 1) * P], ident[:, :])
                    mm.then_inc(L.vT.sem, 1)

                def mixing(m, g):
                    pe.wait_ge(*L.vTl.at(m + 1))
                    for b in range(NBLK):
                        out = ps[:, 6 + b // 4, (b % 4) * P:(b % 4 + 1) * P]
                        for t, (vt, ws) in enumerate(((vt_hi, L.ws_hi), (vt_hi, L.ws_lo), (vt_lo, L.ws_hi))):
                            mm = nc.tensor.matmul(out, vt[:, b, :], ws[:, g, :], start=(t == 0), stop=(t == 2))
                    mm.then_inc(L.mix.sem, 1)

                unit(0, 0, u, r, L.h_hi, L.h_lo)
                pe.wait_ge(*L.vsum_done.at(2 * MA))
                column_sums(L.vsum, L.stat_mm)
                pe.wait_ge(*L.stat.at(1))
                unit(1, 1, u + 1, r + 1, L.h_hi, L.h_lo)
                pe.wait_ge(*L.stat.at(2))
                pe.wait_ge(evac[1], (r + 2) // 2)
                column_sums(ssq, L.stat_mm)

                def body(m, g):
                    even = isinstance(m, int)
                    unit(0, 0, 2 * m + u, r + 2 * m if even else (None, m + r // 2), L.h_hi, L.h_lo)
                    turn(m - 1)
                    unit(1, 1, 2 * m + (u + 1), r + 1 + 2 * m if even else (None, m + r // 2), L.h_hi, L.h_lo)
                    mixing(m - 1, g)

                body(1, 0)
                for g in range(4):
                    with pe.Fori(max(2, 4 * g + 1), min(MA, 4 * g + 5)) as m:
                        body(m, g)
                pe.wait_ge(*L.ws_done.at(1))
                u, r = u + 2 * MA, r + 2 * MA

                def split_done(first):
                    return lambda k: (L.y_odd if k % 2 else L.y_even).at((first + k) // 2 + 1)

                unit(0, 0, u, r, L.y_hi, L.y_lo, split_done(0))
                unit(1, 1, u + 1, r + 1, L.y_hi, L.y_lo)
                turn(MA - 1)
                unit(0, 0, u + 2, r + 2, L.y_hi, L.y_lo)
                mixing(MA - 1, 3)
                unit(1, 1, u + 3, r + 3, L.y_hi, L.y_lo)
                later_units(2, KT, u, r, L.y_hi, L.y_lo)
                u, r = u + KT, r + KT
                units(KT, u, r, Tiles([(L.y_hi, KT + k) for k in range(KT)]),
                      Tiles([(L.y_lo_x, k) if k < A_EARLY else (L.y_lo, k) for k in range(KT)]), split_done(KT))
                post(L, r)

            class Tiles:

                def __init__(self, places):
                    self.places = places

                def __getitem__(self, key):
                    a, k, c_ = key
                    t, m = self.places[k]
                    return t[a, m, c_]

            def layer_b(L):
                u, r = L.u0, L.r0
                first_unit(L)
                unit(1, 1, u + 1, r + 1, L.h_hi, L.h_lo)
                units(2, u + 2, r + 2, L.h_hi, L.h_lo)
                pe.wait_ge(*L.vf_done.at(1))
                pe.wait_ge(*L.rx_done.at(1))
                for b in range(NBLK):
                    mm = nc.tensor.transpose(ps[:, 6 + b // 4, (b % 4) * P:(b % 4 + 1) * P],
                                             L.vf[:, b * P:(b + 1) * P], ident[:, :])
                mm.then_inc(L.v_tr.sem, 1)
                units(2, u + 4, r + 4, L.h_hi, L.h_lo)
                pe.wait_ge(*L.vtok_done.at(1))
                nc.tensor.transpose(ps[0:2 * NS, 6, 0:P], L.vfs[:, :], ident[:, :]).then_inc(L.v_tr.sem, 1)
                units(2 * KT - 4, u + 6, r + 6, L.h_hi, L.h_lo)
                pe.wait_ge(evac[0], (r + 2 * KT + 2) // 2)
                pe.wait_ge(evac[1], (r + 2 * KT + 2) // 2)
                pe.wait_ge(*L.vtok_done.at(2))

                def scores(n, qd, cq):
                    p, kv = qd % 2, qd // 2
                    pe.wait_ge(*L.stq.at(cq + 1))
                    if not (isinstance(cq, int) and cq < 2):
                        pe.wait_ge(*L.B.at(cq - 1))
                    keys = L.kd[:, kv, n * WIN:(n + 2) * WIN] if isinstance(n, int) else L.kd[:, kv, bass.ds(n * WIN, 2 * WIN)]
                    for h in range(4):
                        mm = nc.tensor.matmul(ps[:, 2 * p + h // 2, (h % 2) * 2 * WIN:(h % 2 + 1) * 2 * WIN],
                                              L.qs[:, p, h, :], keys, start=True, stop=True)
                    mm.then_inc(L.S.sem, 1)

                def turns(qd, cq):
                    p = qd % 2
                    pe.wait_ge(*L.C.at(cq + 1))
                    if not (isinstance(cq, int) and cq < 1):
                        pe.wait_ge(*L.PC.at(cq))
                    for h in range(4):
                        for sb_ in range(2):
                            mm = nc.tensor.transpose(ps[:, 4 + sb_, h * P:(h + 1) * P],
                                                     L.sc[:, qd, h, sb_ * WIN:(sb_ + 1) * WIN], ident[:, :])
                    mm.then_inc(L.TP.sem, 1)

                def values(qd, cq):
                    p = qd % 2
                    pe.wait_ge(*L.PC.at(cq + 1))
                    pe.wait_ge(*L.stv.at(cq + 1))
                    if not (isinstance(cq, int) and cq < 2):
                        pe.wait_ge(*L.Dy.at(cq - 1))
                    for sb_ in range(2):
                        mm = nc.tensor.matmul(ps[:, 6 + p, :], L.vs[:, p, sb_, :], L.pt[:, p, sb_, :],
                                              start=(sb_ == 0), stop=(sb_ == 1))
                    mm.then_inc(L.PV.sem, 1)

                def block_step(n, first=False, last=False):
                    for qd in range(4):
                        cq = 4 * n + qd
                        if not (last and qd >= 2):
                            scores(n + (qd + 2) // 4, (qd + 2) % 4, cq + 2)
                        turns(qd, cq)
                        if not (first and qd == 0):
                            values((qd + 3) % 4, cq - 1)

                scores(0, 0, 0)
                scores(0, 1, 1)
                block_step(0, first=True)
                with pe.Fori(1, NBLK - 1) as n:
                    block_step(n)
                block_step(NBLK - 1, last=True)
                values(3, 4 * NBLK - 1)
                pe.wait_ge(*L.zs.at(1))
                pe.wait_ge(*L.PC.at(4 * NBLK))
                pe.wait_ge(*L.B.at(4 * NBLK))
                for e in range(2 * NS):
                    b, kv = e // 2, e % 2
                    mm = nc.tensor.matmul(ps[0:8, e // 3, (e % 3) * (WIN + 1):(e % 3 + 1) * (WIN + 1)],
                                          L.qz[:, b, 8 * kv:8 * kv + 8], L.kc[:, kv, b, :], start=True, stop=True)
                mm.then_inc(L.ssS.sem, 1)
                u, r = u + 2 * KT + 2, r + 2 * KT + 2
                pe.wait_ge(*L.ss_read.at(1))
                pe.wait_ge(w_lo_done, u + 1)
                product(0, u % 2, L.y_hi, L.y_lo, of=(0, 1))
                pe.wait_ge(*L.ssN.at(1))
                pe.wait_ge(*L.Dy.at(4 * NBLK))
                for e in range(2 * NS):
                    nc.tensor.transpose(ps[:, 6, e * 8:(e + 1) * 8], L.ss[0:8, e, 0:WIN], ident[0:8, 0:8])
                nc.tensor.transpose(ps[0:2 * NS, 7, 0:8], L.ss[0:8, :, WIN], ident[0:8, 0:8]).then_inc(L.ssT.sem, 1)
                pe.wait_ge(w_lo_done, u + 2)
                product(1, (u + 1) % 2, L.y_hi, L.y_lo, of=(0,))
                pe.wait_ge(*L.ssP.at(1))
                nc.tensor.matmul(ps[:, 6, 0:P], L.v16[0:2 * NS, :], L.zo[0:2 * NS].rearrange("p a b -> p (a b)"),
                                 start=True, stop=False)
                for b in range(NS):
                    mm = nc.tensor.matmul(ps[:, 6, b * 16:(b + 1) * 16], L.vc[:, b, :], L.pts[:, b * 16:(b + 1) * 16],
                                          start=False, stop=(b == NS - 1))
                mm.then_inc(L.ssO.sem, 1)
                product(1, (u + 1) % 2, L.y_hi, L.y_lo, of=(1,))
                pe.wait_ge(*L.y_lo_done.at(1))
                for j in range(2):
                    product(j, (u + j) % 2, L.y_hi, L.y_lo, of=(2,)).then_inc(result, 1)
                later_units(1, KT, u, r, L.y_hi, L.y_lo)
                post(L, r)

            def layer_c(L):
                u, r = L.u0, L.r0
                first_units(KT, L, L.h_hi, L.h_lo)
                def g_unit(m):
                    r_ = L.g_result(m)
                    u_ = u + KT + 3 * (m // 2) + 2 * (m % 2)
                    unit(u_ % 2, r_ % 2, u_, r_, L.h_hi, L.h_lo)

                def gate_unit(n):
                    u_ = u + KT + 3 * n + 1
                    first = L.result_of(u_) - 3
                    pe.wait_ge(w_lo_done, u_ + 1)
                    pe.wait_ge(*L.xsplit.at(2 * n + 2))
                    for q in range(4):
                        slot = (first + q) % 2
                        pe.wait_ge(evac[slot], (first + q) // 2)
                        for i in range(2):
                            for t, (wt, mv) in enumerate(((w_hi, L.xc_hi[:, i]), (w_hi, L.xc_lo[i]), (w_lo, L.xc_hi[:, i]))):
                                for ch in range(CH):
                                    mm = nc.tensor.matmul(ps[:, 3 * slot + ch, 0:CW], wt[:, u_ % 2, 2 * q + i, :],
                                                          mv[:, ch * CW:(ch + 1) * CW],
                                                          start=(i == 0 and t == 0), stop=(i == 1 and t == 2))
                        mm.then_inc(result, 1)

                for n in range(4):
                    g_unit(2 * n)
                    gate_unit(n)
                    g_unit(2 * n + 1)
                units(KT, u + KT + 12, r + KT + 24, L.y_hi, L.y_lo, lambda k: L.y_lo_done.at(k + 1))
                post(L, r + KT + 24)

            pe.wait_ge(setup, 1)
            for L in layers:
                if L.kind == "a":
                    layer_a(L)
                elif L.kind == "b":
                    layer_b(L)
                else:
                    layer_c(L)

        @block.scalar
        def _(act):
            act.dma_start(g_pre[:], io["g_pre"]).then_inc(gains, 16)
            act.dma_start(ident[:, :], io["ident"]).then_inc(consts, 16)
            act.dma_start(g_post[:], io["g_post"]).then_inc(consts, 16)
            act.dma_start(ln_g[:], io["ln_g"]).then_inc(consts, 16)
            act.dma_start(ln_b[:], io["ln_b"]).then_inc(consts, 16)
            act.dma_start(cvec[:], io["cvec"]).then_inc(consts, 16)

            def pre(L, prev):
                if L.i == 0:
                    act.wait_ge(gains, 16)
                    act.wait_ge(setup, 1)
                for k in range(KT):
                    if prev is None:
                        act.wait_ge(x_in[k], 16)
                    else:
                        act.wait_ge(*prev.x_new.at(k + 1))
                    nc.scalar.activation(L.h_hi[:, k, :], x[:, k, :], ACT.Copy, scale=g_pre[:, L.i, k:k + 1]
                                         ).then_inc(L.hi_done.sem, 1)
                    if k >= 2:
                        act.wait_ge(*L.sq_used.at(k - 1))
                    nc.scalar.activation(sq2[:, k % 2, :], x[:, k, :], ACT.Square).then_inc(L.sq_done.sem, 1)
                    act.dma_start(io["x_save"][k], x[:, k, :]).then_inc(L.x_saved.sem, 16)
                root(L.root, L.ssq_mm, L.rx_done)

            def settle():
                nc.scalar.activation(cell_act[0:1, 0:1], zero[0:1, 0:1], ACT.Copy)
                nc.scalar.drain()

            def read_sums(dst, signal, mm, func, bank=5, **how):
                act.wait_ge(*mm.at(1))
                nc.scalar.activation(dst[:, T:NT], ps[:, bank, 504:512], func, **how)
                nc.scalar.drain().then_inc(signal.sem, 1)
                act.wait_ge(*mm.at(2))
                nc.scalar.activation(dst[:, 0:T].rearrange("p (a b) -> p a b", a=2), ps[:, 6:8, :], func, **how)
                nc.scalar.drain().then_inc(signal.sem, 1)

            def root(signal, mm, done, bank=5):
                read_sums(rx, signal, mm, ACT.Ln, bank, scale=1.0 / D, bias=eps[:, 0:1])
                nc.scalar.activation(rx[:], rx[:], ACT.Exp, scale=-0.5).then_inc(done.sem, 1)

            def x_back(L, tiles=range(KT)):
                for k in tiles:
                    act.dma_start(x[:, k, :], io["x_save"][k]).then_inc(L.x_back.sem, 16)

            def out_single(L, r):
                for m in range(KT):
                    act.wait_ge(result, r + m + 1)
                    nc.scalar.activation(chunks(L.acc[:, m, :]), psum_result((r + m) % 2), ACT.Copy)
                    nc.scalar.drain().then_inc(evac[(r + m) % 2], 1)
                    act.wait_ge(*L.yssq_done.at(m)) if m else None
                    nc.scalar.activation(sqt[:], L.acc[:, m, :], ACT.Square).then_inc(L.ysq_done.sem, 1)
                root(L.yroot, L.yssq_mm, L.rp_done, 2)

            def layer_a(L):
                act.wait_ge(*L.x_saved.at(16 * KT))
                act.wait_ge(*L.h_done.at(KT))
                act.dma_start(L.wsr[:], io["wst"][L.j]).then_inc(L.ws_in.sem, 16)
                act.dma_start(L.tri[:], io["tri"]).then_inc(L.ws_in.sem, 16)
                act.dma_start(bs_bc[:], io["bs"][L.j:L.j + 1].partition_broadcast(P).rearrange("p o g t -> p (o g) t")
                              ).then_inc(L.ws_in.sem, 16)
                act.dma_start(corner[:], io["corner"][L.j:L.j + 1].partition_broadcast(P).rearrange("p o g -> p (o g)")
                              ).then_inc(L.ws_in.sem, 16)
                act.wait_ge(*L.wm.at(1))
                nc.scalar.activation(L.ws_hi[:], L.wsr[:], ACT.Copy).then_inc(L.wh.sem, 1)

                def gelu_v(m, j):
                    act.wait_ge(*L.in_done.at(m + 1))
                    settle()
                    nc.scalar.activation(tile_of(L.v, m), L.tmp[:, j, :], ACT.Gelu_apprx_tanh)
                    nc.scalar.drain().then_inc(L.act_done.sem, 1)
                    if not (isinstance(m, int) and m == 0):
                        act.wait_ge(*L.vsum_done.at(2 * m))
                    settle()
                    nc.scalar.activation(sqt[:], tile_of(L.v, m), ACT.Square).then_inc(L.vsq.sem, 1)

                for j in range(2):
                    gelu_v(j, j)
                with act.Fori(1, MA // 2) as i:
                    for j in range(2):
                        gelu_v(2 * i + j, j)

                def gates(m):
                    act.wait_ge(*L.in_done.at(2 * m + (MA + 1)))
                    nc.scalar.activation(L.tmp[:, 0, :], L.tmp[:, 0, :], ACT.Gelu_apprx_tanh).then_inc(L.u_act.sem, 1)

                def silu(m):
                    act.wait_ge(*L.in_done.at(2 * m + (MA + 2)))
                    nc.scalar.activation(L.tmp[:, 1, :], L.tmp[:, 1, :], ACT.Silu).then_inc(L.g_act.sem, 1)

                def high(m):
                    act.wait_ge(*L.vT.at(m + 1))
                    nc.scalar.activation(vt_hi[:].rearrange("p (a b) n -> p a (b n)", a=2), ps[:, 6:8, :], ACT.Copy
                                         ).then_inc(L.vTh.sem, 1)

                gates(0)
                read_sums(L.mu, L.stat, L.stat_mm, ACT.Copy, scale=1.0 / DA)
                silu(0)
                read_sums(L.rstd, L.stat, Signal(L.stat_mm.sem, L.stat_mm.base + 2), ACT.Copy, scale=1.0 / DA)
                act.wait_ge(*L.var_done.at(1))
                nc.scalar.activation(L.rstd[:], L.rstd[:], ACT.Ln, bias=eps[:, 1:2])
                nc.scalar.drain()
                nc.scalar.activation(L.rstd[:], L.rstd[:], ACT.Exp, scale=-0.5).then_inc(L.stat.sem, 1)

                def body(m):
                    gates(m)
                    high(m - 1)
                    silu(m)

                body(1)
                with act.Fori(2, MA) as m:
                    body(m)
                r = L.r0 + 3 * MA

                def split(m):
                    act.wait_ge(*L.y_done.at(m + 1))
                    if m == 1:
                        act.wait_ge(*L.ug_done.at(1))
                    if m >= 2:
                        act.wait_ge(*L.lo_cut.at(m - 1))
                    nc.scalar.activation(L.y_tmp[m % 2][:], L.y[:, m, :], ACT.Copy).then_inc(L.tmp_hi.sem, 1)

                def in_place(m):
                    act.wait_ge(*L.lo_cut.at(m + 1))
                    nc.scalar.activation(L.y_hi[:, m, :], L.y[:, m, :], ACT.Copy).then_inc(L.y_even.sem, 1)

                def split_all(first, end):
                    split(first)
                    for m in range(first, end):
                        if m + 1 < end:
                            split(m + 1)
                        if m % 2 == 0:
                            in_place(m)

                def evacuate(m):
                    act.wait_ge(result, r + m + 1)
                    nc.scalar.activation(chunks(L.acc[:, m, :]), psum_result(m % 2), ACT.Copy)
                    nc.scalar.drain().then_inc(evac[m % 2], 1)

                act.wait_ge(result, L.r0 + 3 * MA)
                split_all(0, KT)
                evacuate(0)
                evacuate(1)
                high(MA - 1)
                for m in range(2, KT - 1):
                    evacuate(m)
                    if m == 4:
                        split_all(KT, KT + A_EARLY)
                evacuate(KT - 1)
                act.wait_ge(result, L.r0 + 3 * MA + KT)
                split_all(KT + A_EARLY, MA)
                own = range(2, 2 + A_EARLY)
                act.wait_ge(*L.lo_cut.at(MA))
                x_back(L, [k for k in range(KT) if k not in own])
                for m in range(KT):
                    act.wait_ge(*L.acc_done.at(m + 1))
                    act.wait_ge(*L.yssq_done.at(m)) if m else None
                    nc.scalar.activation(sqt[:], L.acc[:, m, :], ACT.Square).then_inc(L.ysq_done.sem, 1)
                x_back(L, own)
                root(L.yroot, L.yssq_mm, L.rp_done, 2)

            def layer_b(L):
                act.wait_ge(*L.x_saved.at(16 * KT))
                act.wait_ge(*L.h_done.at(KT))
                act.dma_start(L.cos[:], io["cos"]).then_inc(L.rope_in.sem, 16)
                act.dma_start(L.sin[:], io["sin"]).then_inc(L.rope_in.sem, 16)
                act.dma_start(L.mask[:], io["mask"]).then_inc(L.rope_in.sem, 16)
                act.dma_start(L.sink[:], io["sink"].partition_broadcast(P).rearrange("p o h -> p (o h)")).then_inc(L.rope_in.sem, 16)

                def swap(src):
                    for a in range(4):
                        b = a ^ 1
                        rows, other = slice(32 * a, 32 * a + 32), slice(32 * b, 32 * b + 32)
                        act.dma_start(L.sw[rows, :], src(other)).then_inc(L.sw_done.sem, 16)

                act.wait_ge(*L.in_done.at(1))
                swap(lambda rows: L.kf[rows, :])
                act.wait_ge(*L.k_rot.at(1))
                for kv in range(2):
                    for half in range(2):
                        nc.scalar.activation(L.kd[64 * half:64 * half + 64, kv, P:P + NT], L.kf[64 * kv:64 * kv + 64, :], ACT.Copy)
                nc.scalar.drain().then_inc(L.kset.sem, 1)
                act.dma_start(io["kp"], L.kf[:, T - WIN:T]).then_inc(L.kout.sem, 16)
                act.dma_start(io["ks"][:, WIN - 1, :], L.kf[:, T:NT]).then_inc(L.kout.sem, 16)
                act.dma_start(io["ks"][:, 0:WIN - 1, :], io["kct"][:, 1:WIN, :]).then_inc(L.kout.sem, 16)
                act.dma_start(io["vs"][:, 0:WIN - 1, :], io["vct"][:, 1:WIN, :]).then_inc(L.kout.sem, 16)
                def q_swap(m):
                    act.wait_ge(*L.in_done.at(m + 3))
                    for a in range(4):
                        b = a ^ 1
                        rows = slice(32 * b, 32 * b + 32)
                        src = L.q[rows, m, :] if isinstance(m, int) else L.q[rows, bass.ds(m, 1), :].rearrange("p o n -> p (o n)")
                        act.dma_start(L.sw[32 * a:32 * a + 32, :], src).then_inc(L.sw_done.sem, 16)

                with act.Fori(0, KT) as m:
                    q_swap(m)
                with act.Fori(0, KT) as m:
                    act.wait_ge(*L.in_done.at(m + (KT + 3)))
                    settle()
                    nc.scalar.activation(tile_of(L.gate, m), L.sw[:], ACT.Silu).then_inc(L.act_done.sem, 1)
                act.wait_ge(result, L.r0 + 2 * KT + 2)
                act.dma_start(L.kc[:, :, :, 0:WIN], io["kcd"]).then_inc(L.at_in.sem, 16)
                act.dma_start(L.vc[:], io["vct"].rearrange("b s f -> s b f")).then_inc(L.at_in.sem, 16)
                act.dma_start(L.sk[0:8, :], io["sink8"]).then_inc(L.at_in.sem, 16)
                act.dma_start(L.dx[0:16], io["dx"]).then_inc(L.at_in.sem, 16)
                act.wait_ge(*L.vtok_done.at(2))
                act.dma_start(io["vp"], L.vtok[:, NBLK, :]).then_inc(L.kout.sem, 16)
                act.dma_start(io["vs"][:, WIN - 1, :], L.v16[0:16:2, :]).then_inc(L.kout.sem, 16)

                def exps(qd, cq):
                    p = qd % 2
                    act.wait_ge(*L.B.at(cq + 1))
                    for h in range(4):
                        nc.scalar.activation(L.sc[:, qd, h, :], L.sc[:, qd, h, :], ACT.Exp, bias=L.mx[:, p, 1, h:h + 1],
                                             accum_out=L.mx[:, p, 2, h:h + 1])
                    nc.scalar.activation(L.mx[:, p, 3, :], L.mx[:, p, 3, :], ACT.Exp)
                    nc.scalar.drain().then_inc(L.X.sem, 1)

                def copies(qd, cq):
                    p = qd % 2
                    act.wait_ge(*L.TP.at(cq + 1))
                    if not (isinstance(cq, int) and cq < 2):
                        act.wait_ge(*L.PV.at(cq - 1))
                    nc.scalar.activation(L.pt[:, p], ps[:, 4:6, :], ACT.Copy).then_inc(L.PC.sem, 1)

                def highs(n, qd, cq):
                    p = qd % 2
                    act.wait_ge(*L.Dy.at(cq + 1))
                    settle()
                    nc.scalar.activation(L.y_hi[:, 2 * qd:2 * qd + 2, bass.ds(n * WIN, WIN) if not isinstance(n, int) else slice(n * WIN, n * WIN + WIN)],
                                         L.yt[:, p], ACT.Copy).then_inc(L.Hh.sem, 1)

                def block_step(n, first=False, last=False):
                    for qd in range(4):
                        cq = 4 * n + qd
                        if not (last and qd == 3):
                            exps((qd + 1) % 4, cq + 1)
                        if not (first and qd < 2):
                            highs(n if qd >= 2 else n - 1, (qd + 2) % 4, cq - 2)
                        copies(qd, cq)

                exps(0, 0)
                block_step(0, first=True)
                with act.Fori(1, NBLK - 1) as n:
                    block_step(n)
                block_step(NBLK - 1, last=True)
                highs(NBLK - 1, 2, 4 * NBLK - 2)
                highs(NBLK - 1, 3, 4 * NBLK - 1)
                act.wait_ge(*L.ssE.at(1))
                nc.scalar.activation(L.ss[0:8], L.ss[0:8], ACT.Exp)
                nc.scalar.activation(L.sm[0:8, 2], L.sm[0:8, 2], ACT.Exp)
                nc.scalar.drain().then_inc(L.ssX.sem, 1)
                act.wait_ge(*L.ssY.at(1))
                nc.scalar.activation(L.y_hi[:, :, T:NT], L.ys[:], ACT.Copy).then_inc(L.ssH.sem, 1)
                act.wait_ge(*L.kout.at(16 * 6))
                x_back(L)
                act.wait_ge(*L.Hh.at(4 * NBLK))
                out_single(L, L.r0 + 2 * KT + 2)

            def layer_c(L):
                act.wait_ge(*L.x_saved.at(16 * KT))
                act.wait_ge(*L.h_done.at(KT))
                act.dma_start(L.st[:, :, 0:CONV - 1, :], io["st"]).then_inc(L.c_in.sem, 16)
                act.dma_start(L.h0[:], io["h0"]).then_inc(L.c_in.sem, 16)
                act.wait_ge(consts, 16 * n_consts)
                nc.scalar.activation(L.sp[:, 0], cvec[:, 7], ACT.Abs)
                nc.scalar.drain()
                nc.scalar.activation(L.sp[:, 0], L.sp[:, 0], ACT.Exp, scale=-1.0).then_inc(L.sp_e.sem, 1)
                act.wait_ge(*L.sp_done.at(1))

                def y_high(m):
                    act.wait_ge(*L.y_done.at(m + 1))
                    nc.scalar.activation(L.y_hi[:, m, :], L.it[:, m % 2, :], ACT.Copy).then_inc(L.y_hi_done.sem, 1)

                def square_root(m):
                    nc.scalar.activation(L.rc[m % 2][:], L.rc[m % 2][:], ACT.Sqrt).then_inc(L.root2.sem, 1)

                def silu(m):
                    act.wait_ge(*L.in_done.at(m + 1))
                    nc.scalar.activation(L.gate[:, m, :], L.gate[:, m, :], ACT.Silu).then_inc(L.g_act.sem, 1)

                def conv_high(n):
                    for t in range(2):
                        nc.scalar.activation(L.xc_hi[:, t, :], L.xc[:, 2 * n + t, :], ACT.Copy).then_inc(L.xh.sem, 1)

                def gate(m, q, dst, vec):
                    res = L.result_of(L.u0 + KT + 3 * (m // 2) + 1) - 3 + 2 * (m % 2) + q
                    act.wait_ge(result, res + 1)
                    nc.scalar.activation(chunks(dst[:, m % 2, :]), psum_result(res % 2), ACT.Sigmoid, bias=cvec[:, vec, m:m + 1])
                    nc.scalar.drain().then_inc(evac[res % 2], 1)

                act.wait_ge(*L.conv_done.at(1))
                conv_high(0)
                silu(0)
                def r_gate(m):
                    if m >= 2:
                        act.wait_ge(*L.used.at(m - 1))
                    gate(m, 0, L.rt, 5)

                def i_gate(m):
                    if m >= 2:
                        act.wait_ge(*L.y_lo_done.at(m - 1))
                    gate(m, 1, L.it, 6)
                    nc.scalar.drain().then_inc(L.sig.sem, 1)

                def tanh(m):
                    nc.scalar.activation(L.rc[m % 2][:], L.rt[:, m % 2, :], ACT.Tanh, scale=L.sp[:, 1, m:m + 1])

                def exp(m):
                    nc.scalar.activation(L.rt[:, m % 2, :], L.rt[:, m % 2, :], ACT.Exp, scale=L.sp[:, 2, m:m + 1])
                    nc.scalar.drain().then_inc(L.th.sem, 1)

                def multiplier(m):
                    act.wait_ge(*L.pm.at(m + 1))
                    square_root(m)

                for n in range(4):
                    last = n == 3
                    m = 2 * n
                    r_gate(m)
                    i_gate(m)
                    if n:
                        y_high(m - 1)
                    r_gate(m + 1)
                    if not last:
                        i_gate(m + 1)
                        for func in (tanh, exp):
                            func(m)
                            func(m + 1)
                        conv_high(n + 1)
                        multiplier(m)
                        multiplier(m + 1)
                    else:
                        tanh(m)
                        exp(m)
                        multiplier(m)
                        i_gate(m + 1)
                        tanh(m + 1)
                        exp(m + 1)
                        multiplier(m + 1)
                    silu(2 * n + 1)
                    y_high(2 * n)
                    silu(2 * n + 2) if not last else y_high(2 * n + 1)
                act.wait_ge(*L.y_lo_done.at(KT))
                act.dma_start(io["ccp"], L.cp[:]).then_inc(L.cout.sem, 16)
                act.dma_start(io["chp"], L.hp[:]).then_inc(L.cout.sem, 16)
                act.dma_start(io["ccs"], L.st[:, :, 1:CONV, :]).then_inc(L.cout.sem, 16)
                act.dma_start(io["chs"], L.hn[:]).then_inc(L.cout.sem, 16)
                act.wait_ge(*L.cout.at(64))
                x_back(L)
                out_single(L, L.r0 + KT + 24)

            prev = None
            for L in layers:
                pre(L, prev)
                (layer_a if L.kind == "a" else layer_b if L.kind == "b" else layer_c)(L)
                if L.kind == "a":
                    act.dma_start(io["av"][L.j], v_new[:]).then_inc(L.vout.sem, 16)
                    act.wait_ge(*L.vout.at(16))
                prev = L
            for k in range(KT):
                act.wait_ge(*prev.x_new.at(k + 1))
                act.dma_start(io["y"][k], x[:, k, :]).then_inc(final, 16)
            act.wait_ge(final, 16 * KT)

        @block.vector
        def _(dve):
            V = nc.vector
            V.memset(zero[:], 0.0)
            V.memset(ones[:], 1.0)
            V.memset(eps[:, 0:1], 1e-6)
            V.memset(eps[:, 1:2], 1e-5)
            V.drain().then_inc(setup, 1)
            dve.wait_ge(gains, 16)

            def pre(L, prev):
                if prev is not None:
                    new_x(prev, 0)
                for k in range(KT):
                    if prev is not None and k + 1 < KT:
                        new_x(prev, k + 1)
                    dve.wait_ge(*L.hi_done.at(k + 1))
                    V.scalar_tensor_tensor(L.h_lo[:, k, :], x[:, k, :], g_pre[:, L.i, k:k + 1], L.h_hi[:, k, :],
                                           ALU.mult, ALU.subtract).then_inc(L.h_done.sem, 1)
                dve.wait_ge(*L.rx_done.at(1))

            def settle():
                V.memset(cell_dve[0:1, 0:1], 0.0)
                V.drain()

            def add_up(total, part, first):
                if first:
                    V.tensor_copy(total[:], part)
                else:
                    V.tensor_tensor(total[:], total[:], part, ALU.add)

            def new_x(L, k):
                if k == 0:
                    dve.wait_ge(*L.rp_done.at(1))
                    V.tensor_tensor(L.acc[:, k, :], L.acc[:, k, :], rx[:], ALU.mult)
                    V.drain()
                    dve.wait_ge(*L.x_back.at(16 * KT))
                else:
                    dve.wait_ge(*L.scaled.at(k))
                V.scalar_tensor_tensor(x[:, k, :], L.acc[:, k, :], g_post[:, L.i, k:k + 1], x[:, k, :], ALU.mult, ALU.add)
                V.drain().then_inc(L.x_new.sem, 1)

            def read(out, slot, r):
                dve.wait_ge(result, r)
                V.tensor_tensor(chunks(out), psum_result(slot), chunks(rx[:]), ALU.mult)
                V.drain().then_inc(evac[slot], 1)

            def yssq(L):
                for m in range(KT - 1):
                    dve.wait_ge(*L.ysq_done.at(m + 1))
                    add_up(ssq, sqt[:], m == 0)
                    V.drain().then_inc(L.yssq_done.sem, 1)

            def layer_a(L):
                r = L.r0
                dve.wait_ge(consts, 16 * n_consts)
                dve.wait_ge(*L.ws_in.at(64))
                for g in range(4):
                    V.tensor_tensor(L.wsr[:, g], L.wsr[:, g], L.tri[:], ALU.mult)
                V.drain().then_inc(L.wm.sem, 1)
                dve.wait_ge(*L.wh.at(1))
                V.tensor_tensor(L.ws_lo[:], L.wsr[:], L.ws_hi[:], ALU.subtract).then_inc(L.ws_done.sem, 1)

                def read_v(m, j):
                    read(L.tmp[:, j, :], j, m + (r + 1))
                    V.drain().then_inc(L.in_done.sem, 1)
                    dve.wait_ge(*L.act_done.at(m + 1))
                    add_up(L.vsum, tile_of(L.v, m), isinstance(m, int) and m == 0)
                    V.drain().then_inc(L.vsum_done.sem, 1)
                    dve.wait_ge(*L.vsq.at(m + 1))
                    add_up(ssq, sqt[:], isinstance(m, int) and m == 0)
                    V.drain().then_inc(L.vsum_done.sem, 1)

                for j in range(2):
                    read_v(j, j)
                with dve.Fori(1, MA // 2) as i:
                    for j in range(2):
                        read_v(2 * i + j, j)
                r += MA

                def read_u(m):
                    read(L.tmp[:, 0, :], 0, 2 * m + (r + 1))
                    V.drain().then_inc(L.in_done.sem, 1)

                def read_g(m):
                    read(L.tmp[:, 1, :], 1, 2 * m + (r + 2))
                    V.drain().then_inc(L.in_done.sem, 1)

                def gated(m):
                    dve.wait_ge(*L.u_act.at(m + 1))
                    dve.wait_ge(*L.g_act.at(m + 1))
                    V.tensor_tensor(L.ug[:], L.tmp[:, 0, :], L.tmp[:, 1, :], ALU.mult)
                    V.drain()

                def normal(m):
                    V.tensor_tensor(L.vstage[:], tile_of(L.v, m), L.mu[:], ALU.subtract)
                    V.drain()
                    V.tensor_tensor(L.vstage[:], L.vstage[:], L.rstd[:], ALU.mult)
                    V.drain()
                    V.tensor_scalar(L.vstage[:], L.vstage[:], col_of(ln_g, L.j, m), col_of(ln_b, L.j, m), ALU.mult, ALU.add)
                    V.drain().then_inc(L.vst.sem, 1)
                    V.tensor_copy(tile_of(v_new, m), L.vstage[:, T:NT])

                def low(m):
                    dve.wait_ge(*L.vTh.at(m + 1))
                    V.tensor_tensor(vt_lo[:].rearrange("p (a b) n -> p a (b n)", a=2), ps[:, 6:8, :],
                                    vt_hi[:].rearrange("p (a b) n -> p a (b n)", a=2), ALU.subtract).then_inc(L.vTl.sem, 1)

                def mixed(m, g):
                    yt = tile_of(L.y, m)
                    dve.wait_ge(*L.mix.at(m + 1))
                    V.tensor_tensor(yt[:, 0:T].rearrange("p (a b) -> p a b", b=P),
                                    ps[:, 6:8, :].rearrange("p a (b n) -> p (a b) n", n=P),
                                    bs_bc[:, g:g + 1, :].to_broadcast([P, NBLK, P]), ALU.add)
                    V.tensor_scalar(yt[:, T:NT], L.vstage[:, T:NT], corner[:, g:g + 1], bs_bc[:, g, 0:1], ALU.mult, ALU.add)
                    V.drain()
                    V.tensor_tensor(yt, yt, L.ug[:], ALU.mult)
                    V.drain().then_inc(L.y_done.sem, 1)

                read_u(0)
                read_g(0)
                dve.wait_ge(*L.stat.at(4))
                V.tensor_tensor(L.vstage[:], L.mu[:], L.mu[:], ALU.mult)
                V.drain()
                V.tensor_tensor(L.rstd[:], L.rstd[:], L.vstage[:], ALU.subtract)
                V.drain()
                V.tensor_scalar(L.rstd[:], L.rstd[:], 0.0, None, ALU.max)
                V.drain().then_inc(L.var_done.sem, 1)
                dve.wait_ge(*L.stat.at(5))
                gated(0)

                def body(m, g):
                    normal(m - 1)
                    read_u(m)
                    low(m - 1)
                    read_g(m)
                    mixed(m - 1, g)
                    gated(m)

                body(1, 0)
                for g in range(4):
                    with dve.Fori(max(2, 4 * g + 1), min(MA, 4 * g + 5)) as m:
                        body(m, g)
                V.drain().then_inc(L.ug_done.sem, 1)

                def cut(m):
                    dve.wait_ge(*L.tmp_hi.at(m + 1))
                    early = KT <= m < KT + A_EARLY
                    V.tensor_tensor(L.y_lo_x[:, m - KT, :] if early else L.y_lo[:, m % KT, :], L.y[:, m, :], L.y_tmp[m % 2][:],
                                    ALU.subtract)
                    V.drain()
                    if m % 2:
                        V.tensor_copy(L.y_hi[:, m, :], L.y_tmp[m % 2][:])
                        V.drain().then_inc(L.y_odd.sem, 1)
                    V.drain().then_inc(L.lo_cut.sem, 1)

                for m in range(KT):
                    cut(m)
                normal(MA - 1)
                low(MA - 1)
                mixed(MA - 1, 3)
                for m in range(KT, 2 * KT):
                    cut(m)
                r += 2 * MA + KT
                for m in range(KT):
                    dve.wait_ge(result, r + m + 1)
                    V.tensor_tensor(chunks(L.acc[:, m, :]), psum_result(m % 2), chunks(L.acc[:, m, :]), ALU.add)
                    V.drain().then_inc(evac[m % 2], 1)
                    V.drain().then_inc(L.acc_done.sem, 1)
                    if m == KT - 1:
                        break
                    dve.wait_ge(*L.ysq_done.at(m + 1))
                    add_up(ssq, sqt[:], m == 0)
                    V.drain().then_inc(L.yssq_done.sem, 1)

            def layer_b(L):
                r = L.r0
                dve.wait_ge(*L.rope_in.at(64))

                def rotate(t, n):
                    dve.wait_ge(*L.sw_done.at(n))
                    V.tensor_tensor(L.sw[:], L.sw[:], L.sin[:], ALU.mult)
                    V.tensor_tensor(t, t, L.cos[:], ALU.mult)
                    V.drain()
                    V.tensor_tensor(t, t, L.sw[:], ALU.add)
                    V.drain()

                read(L.kf[:], 0, r + 1)
                V.drain().then_inc(L.in_done.sem, 1)
                V.memset(L.kd[:, :, 0:P], 0.0)
                V.memset(L.vtok[:, 0, :], 0.0)
                rotate(L.kf[:], 64)
                V.drain().then_inc(L.k_rot.sem, 1)
                read(L.vf[:], 1, r + 2)
                V.tensor_copy(L.vfs[:].rearrange("p (b k) -> p b k", k=2),
                              L.vf[:, T:NT].rearrange("p (b o) -> p b o", o=1).to_broadcast([P, NS, 2]))
                V.drain().then_inc(L.vf_done.sem, 1)
                V.drain().then_inc(L.in_done.sem, 1)
                dve.wait_ge(*L.kset.at(1))

                def read_q(m, slot):
                    read(tile_of(L.q, m), slot, m + (r + 3))
                    V.drain().then_inc(L.in_done.sem, 1)
                    rotate(tile_of(L.q, m), 64 * m + 128)

                for m in range(2):
                    read_q(m, m)
                dve.wait_ge(*L.v_tr.at(1))
                V.tensor_copy(L.vtok[:, 1:NBLK + 1, :], ps[:, 6:8, :].rearrange("p a (b n) -> p (a b) n", n=P))
                V.drain().then_inc(L.vtok_done.sem, 1)
                for m in range(2, 4):
                    read_q(m, m % 2)
                dve.wait_ge(*L.v_tr.at(2))
                V.tensor_copy(L.v16[0:2 * NS, :], ps[0:2 * NS, 6, 0:P])
                V.drain().then_inc(L.vtok_done.sem, 1)
                with dve.Fori(2, KT // 2) as i:
                    for j in range(2):
                        read_q(2 * i + j, j)
                with dve.Fori(0, KT // 2) as i:
                    for j in range(2):
                        read(L.sw[:], j, 2 * i + (r + KT + 3 + j))
                        V.drain().then_inc(L.in_done.sem, 1)
                        dve.wait_ge(*L.act_done.at(2 * i + (j + 1)))
                dve.wait_ge(result, L.r0 + 2 * KT + 2)

                def cols(n):
                    return slice(n * WIN, (n + 1) * WIN) if isinstance(n, int) else bass.ds(n * WIN, WIN)

                def stage_q(n, qd, cq):
                    p = qd % 2
                    for half in range(2):
                        rows = slice(HD * half, HD * half + HD)
                        V.tensor_copy(L.qs[rows, p, half::2, :], L.q[rows, 2 * qd:2 * qd + 2, cols(n)])
                    V.drain().then_inc(L.stq.sem, 1)

                def stage_v(n, qd, cq):
                    p = qd % 2
                    src = L.vtok[:, n:n + 2, :] if isinstance(n, int) else L.vtok[:, bass.ds(n, 2), :]
                    V.tensor_copy(L.vs[:, p], src).then_inc(L.stv.sem, 1)

                def maxima(n, qd, cq, before=True):
                    p = qd % 2
                    dve.wait_ge(*L.S.at(cq + 1))
                    if not (isinstance(cq, int) and cq < 4):
                        dve.wait_ge(*L.TP.at(cq - 3))
                    settle()
                    which = 0 if (isinstance(n, int) and n == 0) else 1
                    for h in range(4):
                        V.tensor_tensor_reduce(L.sc[:, qd, h, :],
                                               ps[:, 2 * p + h // 2, (h % 2) * 2 * WIN:(h % 2 + 1) * 2 * WIN],
                                               L.mask[:, which, :], SCALE, L.sink[:, 4 * qd + h:4 * qd + h + 1],
                                               ALU.add, ALU.max, L.mx[:, p, 0, h:h + 1])
                    if before:
                        sums((qd + 3) % 4, cq - 1)
                    V.drain()
                    V.tensor_scalar(L.mx[:, p, 1, :], L.mx[:, p, 0, :], -1.0, None, ALU.mult)
                    V.tensor_tensor(L.mx[:, p, 3, :], L.sink[:, 4 * qd:4 * qd + 4], L.mx[:, p, 0, :], ALU.subtract)
                    if before:
                        V.reciprocal(L.rq[:, (qd + 3) % 4], L.rq[:, (qd + 3) % 4])
                    V.drain().then_inc(L.B.sem, 1)
                    if before:
                        V.drain().then_inc(L.Rq.sem, 1)

                def sums(qd, cq):
                    p = qd % 2
                    dve.wait_ge(*L.X.at(cq + 1))
                    V.tensor_tensor(L.rq[:, qd], L.mx[:, p, 2, :], L.mx[:, p, 3, :], ALU.add)

                def outputs(n, qd, cq):
                    p, kv = qd % 2, qd // 2
                    dve.wait_ge(*L.PV.at(cq + 1))
                    src = ps[HD * kv:HD * kv + HD, 6 + p, :].rearrange("p (t r n) -> p t r n", t=2, r=2)
                    for half in range(2):
                        rows = slice(HD * half, HD * half + HD)
                        V.tensor_tensor(L.yt[rows, p], src[:, :, half, :], L.gate[rows, 2 * qd:2 * qd + 2, cols(n)], ALU.mult)
                    V.drain().then_inc(L.Dy.sem, 1)

                def lows(n, qd, cq):
                    p = qd % 2
                    dve.wait_ge(*L.Hh.at(cq + 1))
                    V.tensor_tensor(L.y_lo[:, 2 * qd:2 * qd + 2, cols(n)], L.yt[:, p],
                                    L.y_hi[:, 2 * qd:2 * qd + 2, cols(n)], ALU.subtract)

                def block_step(n, first=False, last=False):
                    for qd in range(4):
                        cq = 4 * n + qd
                        if not (last and qd == 3):
                            maxima(n + (qd + 1) // 4, (qd + 1) % 4, cq + 1)
                        else:
                            sums(qd, cq)
                            V.drain()
                            V.reciprocal(L.rq[:, qd], L.rq[:, qd])
                            V.drain().then_inc(L.Rq.sem, 1)
                        if not (last and qd >= 1):
                            stage_q(n + (qd + 3) // 4, (qd + 3) % 4, cq + 3)
                        if not (first and qd < 2):
                            outputs(n if qd >= 2 else n - 1, (qd + 2) % 4, cq - 2)
                        if not (first and qd == 0):
                            stage_v(n, qd, cq)
                        if not (first and qd < 3):
                            lows(n if qd == 3 else n - 1, (qd + 1) % 4, cq - 3)

                V.memset(L.qs[:], 0.0)
                V.drain()
                stage_q(0, 0, 0)
                stage_q(0, 1, 1)
                stage_v(0, 0, 0)
                maxima(0, 0, 0, before=False)
                stage_q(0, 2, 2)
                block_step(0, first=True)
                with dve.Fori(1, NBLK - 1) as n:
                    block_step(n)
                block_step(NBLK - 1, last=True)
                V.drain()
                outputs(NBLK - 1, 2, 4 * NBLK - 2)
                lows(NBLK - 1, 1, 4 * NBLK - 3)
                V.drain()
                outputs(NBLK - 1, 3, 4 * NBLK - 1)
                lows(NBLK - 1, 2, 4 * NBLK - 2)
                lows(NBLK - 1, 3, 4 * NBLK - 1)
                dve.wait_ge(*L.at_in.at(64))
                V.memset(L.qz[:], 0.0)
                V.drain()
                for half in range(2):
                    rows = slice(HD * half, HD * half + HD)
                    V.tensor_copy(L.qz[rows].rearrange("p b (t r) -> p b t r", r=2)[:, :, :, half],
                                  L.q[rows, :, T:NT].rearrange("p t b -> p b t"))
                V.tensor_copy(L.kc[:, :, :, WIN], L.kd[:, :, P + T:P + NT])
                V.drain().then_inc(L.zs.sem, 1)
                dve.wait_ge(*L.ssS.at(1))
                W1 = WIN + 1
                V.tensor_scalar(L.ss[0:8, 0:15, :].rearrange("p (a b) n -> p a (b n)", b=3), ps[0:8, 0:5, 0:3 * W1],
                                SCALE, None, ALU.mult)
                V.tensor_scalar(L.ss[0:8, 15, :], ps[0:8, 5, 0:W1], SCALE, None, ALU.mult)
                V.drain().then_inc(L.ss_read.sem, 1)
                V.tensor_reduce(L.sm[0:8, 0], L.ss[0:8], AX.X, ALU.max)
                V.drain()
                V.tensor_tensor(L.sm[0:8, 0], L.sm[0:8, 0], L.sk[0:8], ALU.max)
                V.drain()
                V.tensor_tensor(L.ss[0:8], L.ss[0:8], L.sm[0:8, 0].rearrange("p (e o) -> p e o", o=1).to_broadcast([8, 16, W1]),
                                ALU.subtract)
                V.tensor_tensor(L.sm[0:8, 2], L.sk[0:8], L.sm[0:8, 0], ALU.subtract)
                V.drain().then_inc(L.ssE.sem, 1)
                dve.wait_ge(*L.ssX.at(1))
                V.tensor_reduce(L.sm[0:8, 1], L.ss[0:8], AX.X, ALU.add)
                V.drain()
                V.tensor_tensor(L.sm[0:8, 1], L.sm[0:8, 1], L.sm[0:8, 2], ALU.add)
                V.drain()
                V.reciprocal(L.sm[0:8, 3], L.sm[0:8, 1])
                V.drain()
                V.tensor_tensor(L.ss[0:8], L.ss[0:8], L.sm[0:8, 3].rearrange("p (e o) -> p e o", o=1).to_broadcast([8, 16, W1]),
                                ALU.mult)
                V.drain().then_inc(L.ssN.sem, 1)
                dve.wait_ge(*L.ssT.at(1))
                V.tensor_copy(L.pts[:], ps[:, 6, 0:P])
                V.tensor_copy(L.po[0:16], ps[0:16, 7, 0:8])
                V.drain()
                V.tensor_tensor(L.zo[0:16], L.po[0:16].rearrange("p (o h) -> p o h", o=1).to_broadcast([16, 16, NS]),
                                L.dx[0:16], ALU.mult)
                V.drain().then_inc(L.ssP.sem, 1)
                dve.wait_ge(*L.ssO.at(1))
                for kv in range(2):
                    src = ps[HD * kv:HD * kv + HD, 6, 0:P].rearrange("p (b k t r) -> p k r t b", b=NS, k=2, t=4)
                    for half in range(2):
                        rows = slice(HD * half, HD * half + HD)
                        V.tensor_tensor(L.ys[rows, 4 * kv:4 * kv + 4, :], src[:, kv, half], L.gate[rows, 4 * kv:4 * kv + 4, T:NT],
                                        ALU.mult)
                V.drain().then_inc(L.ssY.sem, 1)
                dve.wait_ge(*L.ssH.at(1))
                V.tensor_tensor(L.y_lo[:, :, T:NT], L.ys[:], L.y_hi[:, :, T:NT], ALU.subtract)
                V.drain().then_inc(L.y_lo_done.sem, 1)
                yssq(L)

            def layer_c(L):
                r = L.r0
                dve.wait_ge(*L.sp_e.at(1))
                V.tensor_scalar(L.sp[:, 2], L.sp[:, 0], 2.0, None, ALU.add)
                V.drain()
                V.reciprocal(L.sp[:, 2], L.sp[:, 2])
                V.drain()
                V.tensor_tensor(L.sp[:, 2], L.sp[:, 2], L.sp[:, 0], ALU.mult)
                V.drain()
                V.tensor_tensor(L.sp[:, 3], L.sp[:, 2], L.sp[:, 2], ALU.mult)
                V.memset(L.sp[:, 4], 1.0 / 17)
                V.drain()
                for d in (15, 13, 11, 9, 7, 5, 3, 1):
                    V.tensor_tensor(L.sp[:, 4], L.sp[:, 4], L.sp[:, 3], ALU.mult)
                    V.drain()
                    V.tensor_scalar(L.sp[:, 4], L.sp[:, 4], 1.0 / d, None, ALU.add)
                    V.drain()
                V.tensor_tensor(L.sp[:, 4], L.sp[:, 4], L.sp[:, 2], ALU.mult)
                V.tensor_scalar(L.sp[:, 5], cvec[:, 7], -1.0, 0.0, ALU.mult, ALU.max)
                V.drain()
                V.tensor_scalar(L.sp[:, 4], L.sp[:, 4], 16.0, None, ALU.mult)
                V.drain()
                V.scalar_tensor_tensor(L.sp[:, 1], L.sp[:, 5], 8.0, L.sp[:, 4], ALU.mult, ALU.add)
                V.drain()
                V.tensor_scalar(L.sp[:, 2], L.sp[:, 1], -1.0, None, ALU.mult)
                V.drain().then_inc(L.sp_done.sem, 1)
                V.memset(L.xr[:, 0:CONV - 1], 0.0)
                dve.wait_ge(*L.c_in.at(32))

                def tap(t, m):
                    return col_of(cvec, t, m)

                def conv(m, slot):
                    read(L.xr[:, CONV - 1:CONV - 1 + NT], slot, m + (r + 1))
                    st = L.st[:, m] if isinstance(m, int) else L.st[:, bass.ds(m, 1)].rearrange("p o t b -> p (o t) b")
                    V.tensor_copy(st[:, CONV - 1, :], L.xr[:, CONV - 1 + T:CONV - 1 + NT])
                    V.tensor_copy(tile_of(L.cp, m), L.xr[:, T:T + CONV - 1])
                    out = tile_of(L.xc, m)
                    V.tensor_scalar(out[:, 0:T], L.xr[:, 0:T], tap(0, m), tap(4, m), ALU.mult, ALU.add)
                    V.tensor_scalar(out[:, T:NT], st[:, 0, :], tap(0, m), tap(4, m), ALU.mult, ALU.add)
                    V.drain()
                    for t in range(1, CONV):
                        V.scalar_tensor_tensor(out[:, 0:T], L.xr[:, t:t + T], tap(t, m), out[:, 0:T], ALU.mult, ALU.add)
                        V.scalar_tensor_tensor(out[:, T:NT], st[:, t, :], tap(t, m), out[:, T:NT], ALU.mult, ALU.add)
                        V.drain()

                with dve.Fori(0, KT // 2) as i:
                    for j in range(2):
                        conv(2 * i + j, j)
                V.drain().then_inc(L.conv_done.sem, 1)

                def decay(m):
                    rt, rc = L.rt[:, m % 2, :], L.rc[m % 2]
                    dve.wait_ge(*L.th.at(m + 1))
                    V.tensor_tensor(L.hs[:], rt, rt, ALU.mult)
                    V.drain()
                    V.scalar_tensor_tensor(rc[:], L.hs[:], 1.0, rc[:], ALU.add, ALU.mult)
                    V.drain().then_inc(L.pm.sem, 1)

                def recur(m):
                    rt, it, rc = L.rt[:, m % 2, :], L.it[:, m % 2, :], L.rc[m % 2]
                    dve.wait_ge(*L.root2.at(m + 1))
                    V.memset(rc[:, 0:1], 1.0)
                    V.drain()
                    dve.wait_ge(*L.ix.at(m + 1))
                    V.tensor_tensor(it, it, rc[:], ALU.mult)
                    V.tensor_tensor(L.hs[:, T:NT], rt[:, T:NT], L.h0[:, m, :], ALU.mult)
                    V.drain()
                    V.tensor_tensor_scan(L.hs[:, 0:T], rt[:, 0:T], it[:, 0:T], 0.0, ALU.mult, ALU.add)
                    V.tensor_tensor(L.hs[:, T:NT], L.hs[:, T:NT], it[:, T:NT], ALU.add)
                    V.drain().then_inc(L.used.sem, 1)
                    V.tensor_copy(L.hp[:, m:m + 1], L.hs[:, T - 1:T])
                    V.tensor_copy(L.hn[:, m, :], L.hs[:, T:NT])

                def gated(m):
                    dve.wait_ge(*L.g_act.at(m + 1))
                    V.tensor_tensor(L.it[:, m % 2, :], L.hs[:], L.gate[:, m, :], ALU.mult)
                    V.drain().then_inc(L.y_done.sem, 1)

                def low(m):
                    dve.wait_ge(*L.y_hi_done.at(m + 1))
                    V.tensor_tensor(L.y_lo[:, m, :], L.it[:, m % 2, :], L.y_hi[:, m, :], ALU.subtract)
                    V.drain().then_inc(L.y_lo_done.sem, 1)

                def conv_low(n):
                    for t in range(2):
                        dve.wait_ge(*L.xh.at(2 * n + t + 1))
                        V.tensor_tensor(L.xc_lo[t][:], L.xc[:, 2 * n + t, :], L.xc_hi[:, t, :], ALU.subtract
                                        ).then_inc(L.xsplit.sem, 1)

                def read_g(m):
                    read(L.gate[:, m, :], m % 2, L.g_result(m) + 1)
                    V.drain().then_inc(L.in_done.sem, 1)

                conv_low(0)
                read_g(0)
                for n in range(4):
                    decay(2 * n)
                    if n < 3:
                        decay(2 * n + 1)
                        conv_low(n + 1)
                        read_g(2 * n + 1)
                    recur(2 * n)
                    gated(2 * n)
                    if n < 3:
                        read_g(2 * n + 2)
                    else:
                        decay(2 * n + 1)
                        read_g(2 * n + 1)
                    low(2 * n)
                    recur(2 * n + 1)
                    gated(2 * n + 1)
                    low(2 * n + 1)
                yssq(L)

            prev = None
            for L in layers:
                pre(L, prev)
                (layer_a if L.kind == "a" else layer_b if L.kind == "b" else layer_c)(L)
                prev = L
            for k in range(KT):
                new_x(prev, k)


INS = {
    "xt": (KT, P, NT), "wu": (N_UNITS, P, 8 * P), "ident": (P, P), "tri": (P, P),
    "g_pre": (P, 4, KT), "g_post": (P, 4, KT), "ln_g": (P, 2, MA), "ln_b": (P, 2, MA), "cvec": (P, 8, KT),
    "wst": (2, P, 4, P), "bs": (2, 4, P), "corner": (2, 4),
    "cos": (P, NT), "sin": (P, NT), "sink": (1, NH), "sink8": (8, 2 * NS), "mask": (P, 2, 2 * WIN), "dx": (2 * NS, 2 * NS, NS),
    "kct": (P, WIN, NS), "kcd": (P, 2, NS, WIN), "vct": (NS, WIN, P),
    "st": (P, KT, CONV - 1, NS), "h0": (P, KT, NS),
}
OUTS = {
    "y": (KT, P, NT), "av": (2, P, MA, NS), "kp": (P, WIN), "vp": (WIN, P), "ks": (P, WIN, NS), "vs": (NS, WIN, P),
    "ccp": (P, KT, CONV - 1), "chp": (P, KT), "ccs": (P, KT, CONV - 1, NS), "chs": (P, KT, NS),
}


def shape_constants():
    row = np.arange(P)
    half = HD // 2
    inv = np.float32(10000.0) ** (-np.arange(half, dtype=np.float32) / np.float32(half))
    pos = np.concatenate([np.arange(T), np.full(NS, 1024)]).astype(np.float32)
    angle = (pos[None, :] * inv[row % half][:, None]).astype(np.float32)
    sign = np.where(row % HD < half, -1.0, 1.0).astype(np.float32)[:, None]
    q, s = np.arange(WIN)[:, None], np.arange(2 * WIN)[None, :]
    seen = (s - WIN <= q) & (q - (s - WIN) <= WIN)
    mask = np.stack([np.where(seen & (s >= WIN), 0.0, NEG), np.where(seen, 0.0, NEG)], axis=1)
    return {
        "ident": np.eye(P, dtype=np.float32),
        "tri": (row[:, None] <= row[None, :]).astype(np.float32),
        "cos": np.cos(angle), "sin": np.sin(angle) * sign,
        "mask": mask.astype(np.float32),
        "dx": np.repeat(np.eye(2 * NS, dtype=np.float32)[:, :, None], NS, axis=2),
    }


def by_units(w):
    return w.reshape(8, P, -1, P).transpose(2, 1, 0, 3).reshape(-1, P, 8 * P)


def by_features(v):
    return np.moveaxis(v.reshape(v.shape[:-1] + (-1, P)), -1, 0)


def lay_out(i):
    units = []
    for j, kind in ((0, "a"), (0, "b"), (0, "c"), (1, "a")):
        if kind == "a":
            w = by_units(i["a_w_in"][j])
            u, v, g = w[:MA], w[MA:2 * MA], w[2 * MA:]
            units += [v, np.stack([u, g], axis=1).reshape(-1, P, 8 * P)]
            units += [by_units(i["a_w_out"][j][:D]), by_units(i["a_w_out"][j][D:])]
        elif kind == "b":
            w = by_units(i["b_w_in"][0])
            units += [w[KT:KT + 2], w[:KT], w[KT + 2:], by_units(i["b_w_out"][0])]
        else:
            w = by_units(i["c_w_in"][0])
            ax = np.stack([i["c_w_a"][0], i["c_w_x"][0]]).reshape(2, 4, 2, P, 2, P)
            gates = ax.transpose(1, 3, 4, 0, 2, 5).reshape(4, 1, P, 8 * P)
            g = w[KT:].reshape(4, 2, P, 8 * P)
            units += [w[:KT], np.concatenate([g[:, :1], gates, g[:, 1:]], axis=1).reshape(-1, P, 8 * P)]
            units.append(by_units(i["c_w_out"][0]))
    xall = np.concatenate([i["x_prompt"][0], i["x_sample"][:, 0]], axis=0)
    kct = i["cache_b_k"][0].transpose(2, 3, 0, 1)
    cvec = np.concatenate([i["c_conv_w"][0], i["c_conv_b"], i["c_b_a"], i["c_b_x"], i["c_lam"]], axis=0)
    sinks = i["b_sinks"].reshape(2, 8)
    return {
        "xt": xall.T.reshape(KT, P, NT),
        "wu": np.concatenate(units, axis=0),
        "g_pre": by_features(i["norm_pre"]), "g_post": by_features(i["norm_post"]),
        "ln_g": by_features(i["a_ln_g"]), "ln_b": by_features(i["a_ln_b"]), "cvec": by_features(cvec),
        "wst": i["a_w_s"].transpose(0, 3, 1, 2), "bs": i["a_b_s"], "corner": i["a_w_s"][:, :, 0, 0],
        "sink": i["b_sinks"], "sink8": np.tile(sinks.T, (1, NS)),
        "kct": kct.transpose(0, 1, 3, 2).reshape(P, WIN, NS),
        "kcd": np.concatenate([kct, kct], axis=1).transpose(1, 0, 2, 3),
        "vct": i["cache_b_v"][0].reshape(NS, WIN, P),
        "st": by_features(i["state_c_conv"][0]).transpose(0, 3, 2, 1),
        "h0": by_features(i["state_c_h"][0]).transpose(0, 2, 1),
        **shape_constants(),
    }


def kernel(**inputs):
    import concourse.bacc as bacc
    from concourse.bass_utils import run_bass_kernel_spmd

    nc = bacc.Bacc("TRN2", target_bir_lowering=False, num_devices=1)
    laid = lay_out({k: np.asarray(v) for k, v in inputs.items()})
    io, arrays = {}, {}
    for name, shape in INS.items():
        arrays["in_" + name] = np.ascontiguousarray(laid[name])
        assert arrays["in_" + name].shape == shape, (name, arrays["in_" + name].shape, shape)
        io[name] = nc.dram_tensor("in_" + name, shape, F32, kind="ExternalInput").ap()
    for name, shape in OUTS.items():
        io[name] = nc.dram_tensor("out_" + name, shape, F32, kind="ExternalOutput").ap()
    io["x_save"] = nc.dram_tensor("x_save", (KT, P, NT), F32, kind="Internal").ap()
    build(nc, io)
    run = run_bass_kernel_spmd(nc, [arrays], core_ids=[0])
    o = {name: run.results[0]["out_" + name] for name in OUTS}
    y = o["y"].reshape(D, NT)

    def heads(a):
        return a.reshape(a.shape[:-1] + (NKV, HD))

    return (
        np.ascontiguousarray(y[:, :T].T)[None],
        np.ascontiguousarray(y[:, T:].T)[:, None],
        np.ascontiguousarray(o["av"].transpose(0, 3, 2, 1).reshape(2, NS, 1, DA)),
        np.ascontiguousarray(heads(o["kp"].T)[None, None]),
        np.ascontiguousarray(heads(o["vp"])[None, None]),
        np.ascontiguousarray(heads(o["ks"].transpose(2, 1, 0))[None]),
        np.ascontiguousarray(heads(o["vs"])[None]),
        np.ascontiguousarray(o["ccp"].transpose(2, 1, 0).reshape(1, 1, CONV - 1, D)),
        np.ascontiguousarray(o["chp"].T.reshape(1, 1, D)),
        np.ascontiguousarray(o["ccs"].transpose(3, 2, 1, 0).reshape(1, NS, CONV - 1, D)),
        np.ascontiguousarray(o["chs"].transpose(2, 1, 0).reshape(1, NS, D)),
    )
```
